# Optimizing a Trainium2 kernel written in Bass

```python
import jax, jax.numpy as jnp
from jax import lax
import numpy as np

D_MODEL = 1024
BATCH = 1
SEQ = 256
DEPTH = 2

P_DIM = 256
NORM_EPS = 1e-6

MLA_HEADS = 8
MLA_Q_RANK = 384
MLA_KV_RANK = 256
MLA_NOPE = 64
MLA_ROPE = 32
MLA_V = 64
ROPE_THETA = 10000.0
Q_BLOCK = 128

DIL_CONFIGS = ((128, 1), (512, 4), (2048, 16))
DIL_GROUPS = len(DIL_CONFIGS)
DIL_HEADS_PER_GROUP = 8
DIL_HEADS = DIL_GROUPS * DIL_HEADS_PER_GROUP
DIL_HEAD_DIM = 64
DIL_WIDTH = DIL_HEADS * DIL_HEAD_DIM

D_FF = 3584
N_EXPERTS = 8
TOP_K = 2
D_EXPERT = 3584
N_DENSE_LAYERS = (DEPTH + 1) // 2
N_MOE_LAYERS = DEPTH // 2

IN_WIDTHS = (MLA_Q_RANK, MLA_KV_RANK, MLA_ROPE, DIL_WIDTH, DIL_WIDTH, DIL_WIDTH, D_MODEL, D_MODEL)
D_IN = sum(IN_WIDTHS)

kernel_name = "hybrid_mla_dilated_moe_ple"

def rms_norm(x, g):
    xf = x.astype(jnp.float32)
    y = xf * lax.rsqrt(jnp.mean(xf * xf, axis=-1, keepdims=True) + NORM_EPS)
    return (y * g.astype(jnp.float32)).astype(x.dtype)

def rope(x, pos):
    half = x.shape[-1] // 2
    inv_freq = ROPE_THETA ** (-jnp.arange(half, dtype=jnp.float32) / half)
    ang = pos.astype(jnp.float32)[..., None] * inv_freq
    ang = ang.reshape(ang.shape[:2] + (1,) * (x.ndim - 3) + (half,))
    cos, sin = jnp.cos(ang), jnp.sin(ang)
    xf = x.astype(jnp.float32)
    x1, x2 = xf[..., :half], xf[..., half:]
    return jnp.concatenate([x1 * cos - x2 * sin, x2 * cos + x1 * sin], axis=-1).astype(x.dtype)

def alibi_slopes(n):
    def pow2(m):
        start = 2.0 ** (-8.0 / m)
        return [start ** (i + 1) for i in range(m)]
    if float(np.log2(n)).is_integer():
        s = pow2(n)
    else:
        c = 2 ** int(np.floor(np.log2(n)))
        s = pow2(c) + pow2(2 * c)[0::2][: n - c]
    return jnp.asarray(sorted(s, reverse=True), dtype=jnp.float32)

def mla_attention(q_nope, q_rope, k_nope, k_rope, v):
    B, S, H, _ = q_nope.shape
    nb = S // Q_BLOCK
    scale = (MLA_NOPE + MLA_ROPE) ** -0.5
    kpos = jnp.arange(S)

    def one_block(args):
        qn, qr, start = args
        s = (jnp.einsum('bqhd,bkhd->bhqk', qn, k_nope, preferred_element_type=jnp.float32)
             + jnp.einsum('bqhd,bkd->bhqk', qr, k_rope, preferred_element_type=jnp.float32)) * scale
        qpos = start + jnp.arange(Q_BLOCK)
        s = jnp.where(kpos[None, :] <= qpos[:, None], s, -jnp.inf)
        prob = jax.nn.softmax(s, axis=-1)
        return jnp.einsum('bhqk,bkhd->bqhd', prob.astype(v.dtype), v)

    to_blocks = lambda t: t.reshape((B, nb, Q_BLOCK) + t.shape[2:]).swapaxes(0, 1)
    out = lax.map(one_block, (to_blocks(q_nope), to_blocks(q_rope), jnp.arange(nb) * Q_BLOCK))
    return out.swapaxes(0, 1).reshape(B, S, H, MLA_V)

def dilated_group(q, k, v, slopes, window, dilation):
    B, S, H, D = q.shape
    span = window // dilation
    L = S // dilation
    nb = -(-L // span)
    Lp = nb * span
    z = B * dilation

    def to_phase(t):
        t = t.reshape(B, L, dilation, H, D).transpose(0, 2, 1, 3, 4).reshape(z, L, H, D)
        t = jnp.pad(t, ((0, 0), (0, Lp - L), (0, 0), (0, 0)))
        return t.reshape(z, nb, span, H, D)

    def with_prev(t):
        prev = jnp.pad(t[:, :-1], ((0, 0), (1, 0), (0, 0), (0, 0), (0, 0)))
        return jnp.concatenate([prev, t], axis=2)

    qb = to_phase(q)
    kw, vw = with_prev(to_phase(k)), with_prev(to_phase(v))
    s = jnp.einsum('znqhd,znkhd->znhqk', qb, kw, preferred_element_type=jnp.float32) * (D ** -0.5)
    qi = jnp.arange(span)[:, None]
    kj = jnp.arange(2 * span)[None, :]
    dist = qi + span - kj
    blk = jnp.arange(nb)[:, None, None]
    valid = (dist >= 0) & (dist <= span) & (blk * span - span + kj >= 0)
    bias = -slopes[:, None, None] * (dilation * dist).astype(jnp.float32)
    s = jnp.where(valid[None, :, None], s + bias, -jnp.inf)
    m = jnp.max(s, axis=-1, keepdims=True)
    e = jnp.exp(s - m)
    den = jnp.sum(e, axis=-1, keepdims=True)
    o = jnp.einsum('znhqk,znkhd->znqhd', (e / den).astype(vw.dtype), vw)
    lse = (m + jnp.log(den))[..., 0]
    o = o.reshape(B, dilation, Lp, H, D)[:, :, :L].transpose(0, 2, 1, 3, 4).reshape(B, S, H, D)
    lse = lse.transpose(0, 1, 3, 2).reshape(B, dilation, Lp, H)[:, :, :L]
    lse = lse.transpose(0, 2, 1, 3).reshape(B, S, H)
    return o, lse

def dilated_mixer(q, k, v):
    slopes = alibi_slopes(DIL_HEADS)
    outs, lses = [], []
    for g, (window, dilation) in enumerate(DIL_CONFIGS):
        sl = slice(g * DIL_HEADS_PER_GROUP, (g + 1) * DIL_HEADS_PER_GROUP)
        o, l = dilated_group(q[:, :, sl], k[:, :, sl], v[:, :, sl], slopes[sl], window, dilation)
        outs.append(o)
        lses.append(l)
    wts = jax.nn.softmax(jnp.stack(lses, axis=0), axis=0)
    comb = jnp.sum(wts[..., None] * jnp.stack(outs, 0).astype(jnp.float32), axis=0)
    return comb.astype(q.dtype)

def swiglu(h, w_gate, w_up, w_down):
    return (jax.nn.silu(h @ w_gate) * (h @ w_up)) @ w_down

def moe_swiglu(h, w_router, b_router, w_gate, w_up, w_down):
    logits = (h @ w_router).astype(jnp.float32) + b_router.astype(jnp.float32)
    top_val, top_idx = lax.top_k(logits, TOP_K)
    top_w = jax.nn.softmax(top_val, axis=-1)
    gates = jnp.sum(jax.nn.one_hot(top_idx, N_EXPERTS, dtype=jnp.float32) * top_w[..., None], axis=-2)
    out = jnp.zeros(h.shape, jnp.float32)
    for e in range(N_EXPERTS):
        out = out + gates[..., e:e + 1] * swiglu(h, w_gate[e], w_up[e], w_down[e]).astype(jnp.float32)
    return out.astype(h.dtype)

def setup_inputs(seed: int = 0) -> dict:
    key = jax.random.key(seed)
    keys = jax.random.split(key, 32)
    counter = iter(range(32))
    nk = lambda: keys[next(counter)]
    w = lambda shape, fan_in: jax.random.normal(nk(), shape, jnp.float32) * (fan_in ** -0.5)
    gain = lambda shape: 1.0 + 0.05 * jax.random.normal(nk(), shape, jnp.float32)
    start = jax.random.randint(nk(), (BATCH, 1), 0, 1024, dtype=jnp.int32)
    positions = start + jnp.arange(SEQ, dtype=jnp.int32)[None, :]
    return {
        "x": jax.random.normal(nk(), (BATCH, SEQ, D_MODEL), jnp.float32),
        "p": jax.random.normal(nk(), (DEPTH, BATCH, SEQ, P_DIM), jnp.float32),
        "positions": positions,
        "attn_norm": gain((DEPTH, D_MODEL)),
        "w_in": w((DEPTH, D_MODEL, D_IN), D_MODEL),
        "q_norm": gain((DEPTH, MLA_Q_RANK)),
        "w_uq": w((DEPTH, MLA_Q_RANK, MLA_HEADS * (MLA_NOPE + MLA_ROPE)), MLA_Q_RANK),
        "kv_norm": gain((DEPTH, MLA_KV_RANK)),
        "w_ukv": w((DEPTH, MLA_KV_RANK, MLA_HEADS * (MLA_NOPE + MLA_V)), MLA_KV_RANK),
        "w_br_mla": w((DEPTH, MLA_HEADS * MLA_V, D_MODEL), MLA_HEADS * MLA_V),
        "w_br_dil": w((DEPTH, DIL_HEADS_PER_GROUP * DIL_HEAD_DIM, D_MODEL), DIL_HEADS_PER_GROUP * DIL_HEAD_DIM),
        "w_out": w((DEPTH, D_MODEL, D_MODEL), D_MODEL),
        "ffn_norm": gain((DEPTH, D_MODEL)),
        "dense_w_gate": w((N_DENSE_LAYERS, D_MODEL, D_FF), D_MODEL),
        "dense_w_up": w((N_DENSE_LAYERS, D_MODEL, D_FF), D_MODEL),
        "dense_w_down": w((N_DENSE_LAYERS, D_FF, D_MODEL), D_FF),
        "router_w": w((N_MOE_LAYERS, D_MODEL, N_EXPERTS), D_MODEL),
        "router_b": 0.01 * jax.random.normal(nk(), (N_MOE_LAYERS, N_EXPERTS), jnp.float32),
        "moe_w_gate": w((N_MOE_LAYERS, N_EXPERTS, D_MODEL, D_EXPERT), D_MODEL),
        "moe_w_up": w((N_MOE_LAYERS, N_EXPERTS, D_MODEL, D_EXPERT), D_MODEL),
        "moe_w_down": w((N_MOE_LAYERS, N_EXPERTS, D_EXPERT, D_MODEL), D_EXPERT),
        "ple_norm": gain((DEPTH, D_MODEL)),
        "ple_w_gate": w((DEPTH, D_MODEL, D_MODEL), D_MODEL),
        "ple_w_proj": w((DEPTH, P_DIM, D_MODEL), P_DIM),
        "final_norm": gain((D_MODEL,)),
    }

def reference(x, p, positions, attn_norm, w_in, q_norm, w_uq, kv_norm, w_ukv, w_br_mla, w_br_dil,
              w_out, ffn_norm, dense_w_gate, dense_w_up, dense_w_down, router_w, router_b,
              moe_w_gate, moe_w_up, moe_w_down, ple_norm, ple_w_gate, ple_w_proj, final_norm):
    B, S, _ = x.shape
    split_at = tuple(int(o) for o in np.cumsum(IN_WIDTHS)[:-1])
    for i in range(DEPTH):
        h = rms_norm(x, attn_norm[i])
        c_q, c_kv, k_r, q_d, k_d, v_d, g_mla, g_dil = jnp.split(h @ w_in[i], split_at, axis=-1)

        q = (rms_norm(c_q, q_norm[i]) @ w_uq[i]).reshape(B, S, MLA_HEADS, MLA_NOPE + MLA_ROPE)
        q_nope, q_rope = q[..., :MLA_NOPE], rope(q[..., MLA_NOPE:], positions)
        kv = (rms_norm(c_kv, kv_norm[i]) @ w_ukv[i]).reshape(B, S, MLA_HEADS, MLA_NOPE + MLA_V)
        k_nope, v_mla = kv[..., :MLA_NOPE], kv[..., MLA_NOPE:]
        k_rope = rope(k_r, positions)
        o_mla = mla_attention(q_nope, q_rope, k_nope, k_rope, v_mla).reshape(B, S, -1)

        shp = (B, S, DIL_HEADS, DIL_HEAD_DIM)
        o_dil = dilated_mixer(q_d.reshape(shp), k_d.reshape(shp), v_d.reshape(shp)).reshape(B, S, -1)

        merged = (jax.nn.sigmoid(g_mla) * (o_mla @ w_br_mla[i])
                  + jax.nn.sigmoid(g_dil) * (o_dil @ w_br_dil[i]))
        x = x + merged @ w_out[i]

        h = rms_norm(x, ffn_norm[i])
        j = i // 2
        if i % 2 == 0:
            x = x + swiglu(h, dense_w_gate[j], dense_w_up[j], dense_w_down[j])
        else:
            x = x + moe_swiglu(h, router_w[j], router_b[j], moe_w_gate[j], moe_w_up[j], moe_w_down[j])

        h = rms_norm(x, ple_norm[i])
        x = x + jax.nn.sigmoid(h @ ple_w_gate[i]) * (p[i] @ ple_w_proj[i])
    return rms_norm(x, final_norm)


_drawn_inputs = setup_inputs


def setup_inputs(seed=0):
    import zlib

    import numpy as np

    out = dict(_drawn_inputs(seed))
    spreads = {}
    factors = {'q_norm': 4.904, 'kv_norm': 3.171, 'router_b': 22.25, 'ple_norm': 3.361}
    for name, (base, spread) in spreads.items():
        noise = np.random.default_rng([zlib.crc32(name.encode()), seed]).standard_normal(out[name].shape)
        drawn = base * np.exp(spread * noise) if base else spread * noise
        out[name] = __import__('jax').numpy.asarray(drawn.astype(out[name].dtype))
    for name, factor in factors.items():
        out[name] = (out[name] * factor).astype(out[name].dtype)
    return out
```

```python
from contextlib import ExitStack

import numpy as np
import concourse.bass as bass
from concourse import mybir

F32 = mybir.dt.float32
F32R = mybir.dt.float32r
I32 = mybir.dt.int32
U32 = mybir.dt.uint32
ALU = mybir.AluOpType
ACT = mybir.ActivationFunctionType
AX = mybir.AxisListType

P = 128
D = 1024
S = 256
T = S // P
KD = D // P
CH = 512
EPS = 1e-6
QR, KVR, ROPE, NOPE, VD, MH = 384, 256, 32, 64, 64, 8
HQK = NOPE + ROPE
LAT = QR + KVR
KQ, KKV = QR // P, KVR // P
DG, DH = 3, 8
DW = DG * DH * 64
FF = 3584
NF = FF // CH
NE = 8
PD = 256
BIG = 1e30

SLAB, UNIT = 2048, 1024
RAW, RING = 6, 4
UPF = 12
UPE = UPF * NF

U_L0, U_L1, U_V, U_UQ, U_UKV, U_Q, U_K = 0, 4, 6, 18, 22, 24, 36
U_G, U_BM, U_BD, U_O, U_FF = 48, 64, 68, 72, 80
LBASE = [0, U_FF + UPE + 10]
FF0 = [b + U_FF for b in LBASE]
PLE0 = [FF0[0] + UPE, FF0[1] + UPE * NE]

EV_OPS = [2] * 7 + [4, 4] + [2] * 9
GATE_BANKS = (3, 7)
BRANCH_BANKS = ((2, 6), (0, 1))
EV_ACT = [sum(EV_OPS[:n + 1]) for n in range(18)]

MLA_BATCHES = [(0, 0, 4), (0, 4, 4), (1, 0, 2), (1, 2, 2), (1, 4, 2), (1, 6, 2)]
DIL_BATCHES = [(t, h) for h in range(DH) for t in range(T)]
NB_M = len(MLA_BATCHES)
NB = NB_M + len(DIL_BATCHES)
GATE_AT = {n + 2: n for n in range(4)}
GATE_AT.update({NB_M + 2 + 2 * k: 4 + k for k in range(8)})
GATE_AT[NB + 1] = 12
SPLIT_AT = {2: 1, NB_M + 4: 2, NB_M + 8: 3}


def alibi_slopes(n):
    def pow2(m):
        return [(2.0 ** (-8.0 / m)) ** (i + 1) for i in range(m)]
    c = 2 ** int(np.floor(np.log2(n)))
    s = pow2(n) if c == n else pow2(c) + pow2(2 * c)[0::2][:n - c]
    return sorted(s, reverse=True)


ROUNDS_AFTER = [[], [("qk", 0), ("mq", 0), ("mq", 1)], [("qk", 1), ("mk", 0), ("mk", 1)], [("qk", 2)],
                [("qk", 3)], [("qk", 4), ("qk", 5)]]
CHUNK_ROUND = [0, 3, 6, 7, 8, 9]

SLOPES = alibi_slopes(DG * DH)


def trunk_kernel(nc, x, p, positions, attn_norm, w_in, q_norm, w_uq, kv_norm, w_ukv, w_br_mla, w_br_dil,
                 w_out, ffn_norm, dense_w_gate, dense_w_up, dense_w_down, router_w, router_b,
                 moe_w_gate, moe_w_up, moe_w_down, ple_norm, ple_w_gate, ple_w_proj, final_norm, out):
    ctx = ExitStack()
    with ctx:
        ctx.enter_context(nc.allow_non_contiguous_dma(reason="small transposing loads of positions"))
        base = (nc.sbuf_base + 63) // 64 * 64
        arena = ctx.enter_context(nc.sbuf_tensor("arena", [P, (nc.sbuf_usable_end - base) // 4 - 64], F32))
        del arena
        top = [base]

        def at(name, shape, dtype, offset):
            return nc.alloc_sbuf_tensor_at(name, shape, dtype=dtype, offset=offset)

        def sb(name, shape, dtype=F32):
            n = int(np.prod(shape[1:])) * 4
            t = at(name, shape, dtype, top[0])
            top[0] += (n + 31) // 32 * 32
            return t

        def region(n):
            r = top[0]
            top[0] += n
            return r

        raw = sb("raw", [P, RAW, SLAB])
        hi = sb("hi", [P, RING, UNIT], F32R)
        lo = sb("lo", [P, RING, UNIT], F32R)
        xs = sb("xs", [P, T, D])
        hT_hi = sb("hT_hi", [P, KD, S], F32R)
        hT_lo = sb("hT_lo", [P, KD, S], F32R)
        gain = sb("gain", [P, D])
        glat = sb("glat", [P, LAT])
        o_mla = sb("o_mla", [P, T, 512])
        o_dil = sb("o_dil", [P, T, 512])
        ident = sb("ident", [P, P])
        iota = sb("iota", [P, P])
        cmask = sb("cmask", [P, 256])
        dist = sb("dist", [P, DG, 256])
        upper = sb("upper", [P, P])
        ones = sb("ones", [P, P])
        cos = sb("cos", [P, T, 16])
        sin = sb("sin", [P, T, 16])
        ss = sb("ss", [P, 8])
        ms = sb("ms", [P, 8])
        rstd = sb("rstd", [P, 8])
        nhalf = sb("nhalf", [P, 8])
        part = sb("part", [P, 2])
        nmax = sb("nmax", [P, 2, 4])
        sums = sb("sums", [P, 2, 4])
        rsum = sb("rsum", [P, 2, 4])
        krope = sb("krope", [P, T, ROPE])
        qk_odd = region(6144)
        Dr = region(36864)
        Mr = region(20480)
        Tr = region(20480)
        assert top[0] <= nc.sbuf_usable_end, (top[0], nc.sbuf_usable_end)
        qT = at("qT", [P, 12, S], F32, Dr)
        kT = at("kT", [P, 12, S], F32, Dr + 12288)
        vd = at("vd", [P, T, DW], F32, Dr + 24576)
        qT_lo = at("qT_lo", [P, 12, S], F32R, Dr)
        kT_lo = at("kT_lo", [P, 12, S], F32R, Dr + 12288)
        qnat = at("qnat", [P, T, MH, HQK], F32, Dr + 6144)
        knat = at("knat", [P, T, MH, HQK], F32, Dr + 12288)
        omT_hi = at("omT_hi", [P, 4, S], F32R, Dr)
        omT_lo = at("omT_lo", [P, 4, S], F32R, Dr + 4096)
        odT_hi = at("odT_hi", [P, 4, S], F32R, Dr + 8192)
        odT_lo = at("odT_lo", [P, 4, S], F32R, Dr + 12288)
        merged = at("merged", [P, T, D], F32, Dr + 16384)
        qmT = at("qmT", [P, MH, S], F32, Mr)
        kmT = at("kmT", [P, MH, S], F32, Mr + 8192)
        vm = at("vm", [P, T, MH, VD], F32, Mr + 16384)
        gates = at("gates", [P, 2, T, D], F32, Mr)
        hnat = at("hnat", [P, T, D], F32, Tr)
        lat = at("lat", [P, T, LAT + ROPE], F32, Tr)
        latT_hi = at("latT_hi", [P, KQ + KKV, S], F32R, Tr + 5376)
        latT_lo = at("latT_lo", [P, KQ + KKV, S], F32R, Tr + 10496)
        rt = at("rt", [P, 4, MH, 16], F32, Tr + 15616)
        chunk = at("chunk", [P, 2, T, CH], F32, Tr)
        pr = at("pr", [P, 2, 768], F32, Tr + 8192)
        pT = at("pT", [P, 2, 6, P], F32, Tr + 14336)
        qk_hi = [at(f"qk_hi{j}", [P, 2, DG, S], F32R, o) for j, o in enumerate((Tr, qk_odd))]
        dint = at("dint", [P, 256], I32, Mr)
        dand = at("dand", [P, 256], I32, Mr + 1024)
        dflt = at("dflt", [P, 256], F32, Mr + 2048)
        dmod = at("dmod", [P, 256], F32, Mr + 3072)
        posi = at("posi", [P, T], I32, Mr + 4096)
        posf = at("posf", [P, T], F32, Mr + 4160)
        ang = at("ang", [P, T, 16], F32, Mr + 4224)
        freq = at("freq", [P, 16], F32, Mr + 4352)
        kq = at("kq", [P, T, 16], F32, Mr + 4416)
        sh = at("sh", [P, T, 16], F32, Mr + 4544)
        iint = at("iint", [P, P], I32, Mr + 4672)
        f_sig = at("f_sig", [P, T, CH], F32, Dr)
        f_act = at("f_act", [P, T, CH], F32, Dr + 4096)
        faT_hi = at("faT_hi", [P, 4, S], F32R, Dr + 8192)
        faT_lo = at("faT_lo", [P, 4, S], F32R, Dr + 12288)
        hn_hi = at("hn_hi", [P, T, D], F32R, Dr)
        hn_lo = at("hn_lo", [P, T, D], F32R, Dr + 8192)
        hs_hi = at("hs_hi", [P, KD, P], F32R, Dr + 16384)
        hs_lo = at("hs_lo", [P, KD, P], F32R, Dr + 20480)
        e_sig = at("e_sig", [P, CH], F32, Dr + 24576)
        e_act = at("e_act", [P, CH], F32, Dr + 26624)
        eaT_hi = at("eaT_hi", [P, 4, P], F32R, Dr + 28672)
        eaT_lo = at("eaT_lo", [P, 4, P], F32R, Dr + 30720)
        y_hi = at("y_hi", [P, D], F32R, Dr + 32768)
        y_lo = at("y_lo", [P, D], F32R, Dr + 36864)
        sel = at("sel", [P, T, P], F32R, Dr + 40960)
        selT = at("selT", [P, S], F32R, Dr + 41984)
        rt0 = Dr + 43008
        rw = at("rw", [P, KD, NE], F32, rt0)
        rw_hi = at("rw_hi", [P, KD, NE], F32R, rt0 + 256)
        rw_lo = at("rw_lo", [P, KD, NE], F32R, rt0 + 512)
        rb = at("rb", [P, NE], F32, rt0 + 768)
        lg = at("lg", [P, T, NE], F32, rt0 + 800)
        mx8 = at("mx8", [P, T, 8], F32, rt0 + 864)
        ix8 = at("ix8", [P, T, 8], U32, rt0 + 928)
        ixf = at("ixf", [P, T, 8], F32, rt0 + 992)
        oh1 = at("oh1", [P, T, NE], F32, rt0 + 1056)
        oh2 = at("oh2", [P, T, NE], F32, rt0 + 1120)
        mask = at("mask", [P, T, NE], F32, rt0 + 1184)
        gts = at("gts", [P, T, NE], F32, rt0 + 1248)
        slot = at("slot", [P, T, NE], F32, rt0 + 1312)
        dv = at("dv", [P, T], F32, rt0 + 1376)
        w12 = at("w12", [P, 2, T], F32, rt0 + 1408)
        tot = at("tot", [P, 1], F32, rt0 + 1440)
        npass = at("npass", [1, 1], I32, rt0 + 1472)
        gcol = at("gcol", [P, T], F32, rt0 + 1504)
        gslot = at("gslot", [P, 1], F32, rt0 + 1536)
        pnat = at("pnat", [P, T, PD], F32, Dr + 49152)
        peT_hi = at("peT_hi", [P, 2, S], F32R, Dr + 51200)
        peT_lo = at("peT_lo", [P, 2, S], F32R, Dr + 53248)
        psg = at("psg", [P, T, D], F32, Dr)

        ps = ctx.enter_context(nc.psum_tensor("ps", [P, 8, CH], F32))

        def sem(name):
            return ctx.enter_context(nc.semaphore(name))

        raw_in = [sem(f"raw_in{j}") for j in range(RAW)]
        hi_done = sem("hi_done")
        lo_done = sem("lo_done")
        used = sem("used")
        LO0, US0 = 2 * RAW, RING

        x_in, pos_in, const_ok = sem("x_in"), sem("pos_in"), sem("const_ok")
        gain0_in = sem("gain0_in")
        gain_in, glat_in, p_in, rw_in = sem("gain_in"), sem("glat_in"), sem("p_in"), sem("rw_in")
        v_link, g_link = sem("v_link"), sem("g_link")
        ang_ok, trig_ok, rot_ok = sem("ang_ok"), sem("trig_ok"), sem("rot_ok")

        n_sq, n_ms, n_rs, n_hn = sem("n_sq"), sem("n_ms"), sem("n_rs"), sem("n_hn")
        n_tr, n_hi, n_lo = sem("n_tr"), sem("n_hi"), sem("n_lo")

        class Norm:
            def __init__(self, k):
                self.sq = n_sq
                self.hn = n_hn
                self.ms, self.rs, self.k = n_ms, n_rs, k
                self.tr, self.g = n_tr, 4 * k
                self.hi, self.lo = n_hi, n_lo

        class Layer:
            def __init__(self, name, index):
                self.n1, self.nl, self.n2, self.n3 = (Norm(4 * index + k) for k in range(4))
                self.ev_act = sem(name + "ev_act")
                self.ev_vec = sem(name + "ev_vec")
                self.tround = sem(name + "tround")
                self.tevac = sem(name + "tevac")
                self.rope_q = sem(name + "rope_q")
                self.rope_k = sem(name + "rope_k")
                self.qk_hi = sem(name + "qk_hi")
                self.qk_lo = sem(name + "qk_lo")
                self.gsig = sem(name + "gsig")
                self.score = sem(name + "score")
                self.smax = sem(name + "smax")
                self.prob = sem(name + "prob")
                self.ptr = sem(name + "ptr")
                self.ptev = sem(name + "ptev")
                self.pv = sem(name + "pv")
                self.oev = sem(name + "oev")
                self.otr = sem(name + "otr")
                self.ohi = sem(name + "ohi")
                self.olo = sem(name + "olo")
                self.madd = sem(name + "madd")
                self.mtr = sem(name + "mtr")
                self.mhi = sem(name + "mhi")
                self.mlo = sem(name + "mlo")
                self.ptr2 = sem(name + "ptr2")
                self.phi = sem(name + "phi")
                self.plo = sem(name + "plo")
                self.pev_act = sem(name + "pev_act")
                self.pev_vec = sem(name + "pev_vec")
                self.padd = sem(name + "padd")

        layers = [Layer(f"l{i}", i) for i in range(2)]
        nfin = Norm(8)
        f_sigd, f_t1, f_actd, f_tr, f_hi, f_lo, f_xadd = (sem("ff_" + n) for n in
                                                          ("sig", "t1", "act", "tr", "hi", "lo", "xadd"))
        (r_w, r_log, r_v, r_sg, r_msk, r_rank, r_np, hn_h, hn_l) = (sem("r_" + n) for n in (
            "w", "log", "v", "sg", "msk", "rank", "np", "hnh", "hnl"))
        (e_sigd, e_t1, e_actd, e_tr, e_hi, e_lo, e_sel, e_gath, e_hsh, e_hsl, e_st, e_stev, e_yhi, e_ylo,
         e_scat, e_xadd) = (sem("e_" + n) for n in (
             "sig", "t1", "act", "tr", "hi", "lo", "sel", "gath", "hsh", "hsl", "st", "stev", "yhi", "ylo",
             "scat", "xadd"))
        out_done = sem("out_done")

        def tok_blocks(dst, n):
            return dst[:, 0:n, :].rearrange("p k (t j) -> p t k j", t=T)

        def pair_blocks(b0, rows=P):
            return ps[0:rows, b0:b0 + 2, :].rearrange("p t (k j) -> p t k j", j=P)

        def pe_blocks():
            return ps[:, 0, :].rearrange("p (t k j) -> p t k j", t=T, j=P)

        groups = [(t, h) for h in range(2) for t in range(T)]

        def pair_of(src, hp):
            return src[:].rearrange("p (m b) s -> p b m s", b=DH // 2)[:, hp]

        def hT_groups(dst):
            return ([dst[:, 4 * h:4 * h + 4, P * t:P * t + P] for t, h in groups],
                    [ps[:, 4 + j, :].rearrange("p (k q) -> p k q", q=P) for j in range(4)])

        def lat_groups(dst):
            ds, banks = [], []
            for t in range(T):
                for k0, n, bank in ((0, KQ, 4 + 2 * t), (KQ, KKV, 5 + 2 * t)):
                    ds.append(dst[:, k0:k0 + n, P * t:P * t + P])
                    banks.append(ps[:, bank, 0:P * n].rearrange("p (k q) -> p k q", q=P))
            return ds, banks

        def lat_pairs():
            return ([(lat[:, t, 0:QR], pr[:, t, 0:QR]) for t in range(T)]
                    + [(lat[:, t, QR:LAT], pr[:, t, QR:LAT]) for t in range(T)])

        def unit_views(u, src, dst):
            i = 1 if u >= LBASE[1] else 0
            off, h = u - LBASE[i], u % 2
            slab, slot = src[:, (u // 2) % RAW, :], dst[:, u % RING, :]
            if off in (U_L1, U_L1 + 1):
                return slab[:, 640 * h:640 * h + 640], slot[:, 0:640]
            if U_UQ <= off < U_UKV:
                k, w = KQ, 192
            elif U_UKV <= off < U_Q or PLE0[i] <= u < PLE0[i] + 2:
                k, w = 2, CH
            else:
                return slab[:, UNIT * h:UNIT * h + UNIT], slot[:, :]
            return (slab[:, 0:2 * k * w].rearrange("p (k n) -> p k n", k=k)[:, :, w * h:w * h + w],
                    slot[:, 0:k * w].rearrange("p (k n) -> p k n", k=k))

        block = ctx.enter_context(nc.Block())

        @block.sync
        def _(sp):
            sp.dma_start(xs[:], x.rearrange("a (t p) d -> p (a t) d", p=P)).then_inc(x_in, 16)
            sp.dma_start(gain[:], attn_norm[0].partition_broadcast(P)).then_inc(gain0_in, 16)

            def load(s, dst_dims, src, ds=0, dr=0):
                n = dst_dims[0] * dst_dims[1]
                sp.wait_ge(lo_done, ds + 2 * s + 2)
                dst = raw[:, s % RAW, 0:n].rearrange("p (k n) -> p k n", k=dst_dims[0])
                sp.dma_start(dst, src).then_inc(raw_in[s % RAW], 16)

            def gemm_cols(s, w2d, c0, width=CH, ds=0):
                v = w2d.rearrange("(h k p) n -> h p k n", p=P, k=4)
                for h in range(2):
                    load(s + h, (4, width), v[h, :, :, c0:c0 + width], ds)

            def ffn_step(s, wg, wu, wd, f, fd, parts, ds=0):
                if "g" in parts:
                    v = wg.rearrange("(h k p) n -> h p k n", p=P, k=4)
                    for h in range(2):
                        load(s, (4, CH), v[h, :, :, bass.ts(f, CH)], ds)
                        s += 1
                if "d" in parts:
                    vd_ = wd.rearrange("(f k p) n -> f p k n", p=P, k=4)
                    load(s, (4, CH), vd_[fd, :, :, 0:CH], ds)
                    s += 1
                if "g" in parts:
                    v = wu.rearrange("(h k p) n -> h p k n", p=P, k=4)
                    for h in range(2):
                        load(s, (4, CH), v[h, :, :, bass.ts(f, CH)], ds)
                        s += 1
                if "d" in parts:
                    vd_ = wd.rearrange("(f k p) n -> f p k n", p=P, k=4)
                    load(s, (4, CH), vd_[fd, :, :, CH:2 * CH], ds)

            def attn_stream(i):
                b = LBASE[i] // 2
                w = w_in[i]
                gemm_cols(b, w, 0)
                load(b + 2, (8, 160), w.rearrange("(k p) n -> p k n", p=P)[:, :, CH:LAT + ROPE])
                c0 = LAT + ROPE
                for j in range(3):
                    gemm_cols(b + 3 + 2 * j, w, c0 + 2 * DW + CH * j)
                for c in range(2):
                    load(b + 9 + c, (3, 384), w_uq[i].rearrange("(k p) n -> p k n", p=P)[:, :, 384 * c:384 * c + 384])
                load(b + 11, (2, 1024), w_ukv[i].rearrange("(k p) n -> p k n", p=P))
                for j in range(3):
                    gemm_cols(b + 12 + 2 * j, w, c0 + CH * j)
                for j in range(3):
                    gemm_cols(b + 18 + 2 * j, w, c0 + DW + CH * j)
                for j in range(4):
                    gemm_cols(b + 24 + 2 * j, w, c0 + 3 * DW + CH * j)
                for k, wb in enumerate((w_br_mla[i], w_br_dil[i])):
                    for c in range(2):
                        load(b + 32 + 2 * k + c, (4, CH),
                             wb.rearrange("(k p) n -> p k n", p=P)[:, :, CH * c:CH * c + CH])
                for c in range(2):
                    gemm_cols(b + 36 + 2 * c, w_out[i], CH * c)

            def ple_stream(i, ds):
                b = PLE0[i] // 2
                load(b, (2, 1024), ple_w_proj[i].rearrange("(k p) n -> p k n", p=P), ds)
                for c in range(2):
                    gemm_cols(b + 1 + 2 * c, ple_w_gate[i], CH * c, ds=ds)

            attn_stream(0)
            g, u, d = dense_w_gate[0], dense_w_up[0], dense_w_down[0]
            b = FF0[0] // 2
            ffn_step(b, g, u, d, 0, 0, "g")
            with sp.Fori(0, NF - 1) as j:
                ffn_step(b + 4, g, u, d, j + 1, j, "gd", j * UPF)
            ffn_step(b + 40, g, u, d, 0, NF - 1, "d")
            ple_stream(0, 0)
            attn_stream(1)
            b = FF0[1] // 2
            mg, mu, md = moe_w_gate[0], moe_w_up[0], moe_w_down[0]

            def expert(e):
                return (mg[e], mu[e], md[e])

            def experts_stream(dq):
                ffn_step(b, *expert(0), 0, 0, "g", dq)
                ffn_step(b + 4, *expert(0), 1, 0, "gd", dq)
                with sp.Fori(0, NE - 1) as e:
                    dsn = e * UPE + dq
                    ge, ue, de = mg[e], mu[e], md[e]
                    gn, un, dn = mg[e + 1], mu[e + 1], md[e + 1]
                    for f in range(2, NF):
                        ffn_step(b + 10 + 6 * (f - 2), ge, ue, de, f, f - 1, "gd", dsn)
                    ffn_step(b + 40, gn, un, de, 0, NF - 1, "gd", dsn)
                    ffn_step(b + 46, gn, un, dn, 1, 0, "gd", dsn)
                bl = b + 42 * (NE - 1)
                for f in range(2, NF):
                    ffn_step(bl + 10 + 6 * (f - 2), *expert(NE - 1), f, f - 1, "gd", dq)
                ffn_step(bl + 40, *expert(NE - 1), 0, NF - 1, "d", dq)

            experts_stream(0)
            sp.wait_ge(r_np, 1)
            n = sp.value_load(npass[0:1, 0:1], min_val=1, max_val=2)
            with sp.If(n > 1):
                experts_stream(UPE * NE)
            with sp.Else():
                sp.nop()
            ple_stream(1, (n - 1) * (UPE * NE))
            for h in range(2):
                sp.wait_ge(nfin.hn, nfin.g + 2 * h + 2)
                sp.dma_start(out.rearrange("a (t p) d -> p (a t) d", p=P)[:, :, CH * h:CH * h + CH],
                             hnat[:, :, CH * h:CH * h + CH]).then_inc(out_done, 16)
            sp.wait_ge(out_done, 32)

        @block.gpsimd
        def _(g):
            g.sem_inc(lo_done, LO0)
            g.sem_inc(used, US0)
            g.sem_inc(f_xadd, 1)
            g.sem_inc(e_t1, 1)
            g.sem_inc(e_actd, 1)
            g.sem_inc(e_ylo, 2)
            g.sem_inc(e_xadd, 2)
            gl = [0]

            def link(ins):
                gl[0] += 1
                ins.then_inc(g_link, 1)
                g.wait_ge(g_link, gl[0])

            def power(n, w):
                g.wait_ge(n.ms, n.k + 1)
                g.tensor_tensor(rstd[:, 0:w], ms[:, 0:w], nhalf[:, 0:w], ALU.pow).then_inc(n.rs, 1)


            def load_gain(src):
                g.dma_start(gain[:], src.partition_broadcast(P)).then_inc(gain_in, 16)

            link(g.memset(nhalf[:], -0.5))
            link(g.memset(ident[:], 0.0))
            link(g.affine_select(out=ident[:], in_=ident[:], compare_op=ALU.not_equal, fill=1.0, base=0,
                                 pattern=[[-1, P]], channel_multiplier=1))
            g.sem_inc(const_ok, 1)
            g.dma_start(glat[:, 0:QR], q_norm[0].partition_broadcast(P)).then_inc(glat_in, 16)
            g.dma_start(glat[:, QR:LAT], kv_norm[0].partition_broadcast(P)).then_inc(glat_in, 16)
            g.dma_start(posi[:], positions.rearrange("a (t p) -> p (a t)", p=P)).then_inc(pos_in, 16)
            power(layers[0].n1, 2)
            link(g.memset(ones[:], 1.0))
            link(g.affine_select(out=upper[:], in_=ones[:], compare_op=ALU.is_gt, fill=0.0, base=0,
                                 pattern=[[1, P]], channel_multiplier=-1))
            link(g.iota(iint[:], [[1, P]], base=0, channel_multiplier=0))
            link(g.tensor_copy(iota[:], iint[:]))
            link(g.iota(dint[:], [[-1, 256]], base=P, channel_multiplier=1))
            link(g.memset(cmask[:], 0.0))
            link(g.affine_select(out=cmask[:], in_=cmask[:], compare_op=ALU.is_ge, fill=-BIG, base=P,
                                 pattern=[[-1, 256]], channel_multiplier=1))
            for j in range(16):
                g.memset(freq[:, j:j + 1], float(np.float32(10000.0) ** np.float32(-j / 16)))
            link(g.memset(cos[:], 0.0))
            g.sem_inc(const_ok, 1)
            g.wait_ge(layers[0].n1.hn, 4)
            load_gain(ffn_norm[0])
            g.wait_ge(ang_ok, 1)
            for m in range(DG):
                link(g.affine_select(out=dist[:, m, :], in_=dist[:, m, :], compare_op=ALU.is_ge, fill=BIG,
                                     base=P, pattern=[[-1, 256]], channel_multiplier=1))
            link(g.affine_select(out=dist[:, 0, :], in_=dist[:, 0, :], compare_op=ALU.is_ge, fill=BIG,
                                 base=0, pattern=[[1, 256]], channel_multiplier=-1))

            def rotate(dst, t, n):
                x1, x2 = dst[:, :, 0:16], dst[:, :, 16:32]
                c = cos[:, t, :].unsqueeze(1).to_broadcast([P, n, 16])
                s = sin[:, t, :].unsqueeze(1).to_broadcast([P, n, 16])
                g.tensor_tensor(rt[:, 0, 0:n, :], x1, c, ALU.mult)
                g.tensor_tensor(rt[:, 1, 0:n, :], x2, s, ALU.mult)
                g.tensor_tensor(rt[:, 2, 0:n, :], x2, c, ALU.mult)
                link(g.tensor_tensor(rt[:, 3, 0:n, :], x1, s, ALU.mult))
                g.tensor_tensor(x1, rt[:, 0, 0:n, :], rt[:, 1, 0:n, :], ALU.subtract)
                link(g.tensor_tensor(x2, rt[:, 2, 0:n, :], rt[:, 3, 0:n, :], ALU.add))

            for i in range(2):
                y = layers[i]
                if i:
                    power(y.n1, 2)
                if i:
                    g.wait_ge(y.n1.hn, y.n1.g + 4)
                    load_gain(ffn_norm[i])
                power(y.nl, 4)
                if i == 0:
                    g.wait_ge(rot_ok, 1)
                g.wait_ge(y.ev_act, EV_ACT[1])
                for t in range(T):
                    link(g.tensor_copy(krope[:, t, :], lat[:, t, LAT:LAT + ROPE]))
                    rotate(krope[:, t, :].unsqueeze(1), t, 1)
                g.wait_ge(y.ev_act, EV_ACT[6])
                for t in range(T):
                    rotate(qnat[:, t, :, NOPE:HQK], t, MH)
                g.sem_inc(y.rope_q, 1)
                for t in range(T):
                    link(g.tensor_copy(knat[:, t, :, NOPE:HQK], krope[:, t, :].unsqueeze(1).to_broadcast([P, MH, ROPE])))
                g.sem_inc(y.rope_k, 1)
                g.wait_ge(y.nl.hn, y.nl.g + 4)
                if i == 0:
                    g.dma_start(glat[:, 0:QR], q_norm[1].partition_broadcast(P)).then_inc(glat_in, 16)
                    g.dma_start(glat[:, QR:LAT], kv_norm[1].partition_broadcast(P)).then_inc(glat_in, 16)
                for c in range(2):
                    for t in range(T):
                        g.wait_ge(y.ev_vec, 4 + 2 * c + t + 1)
                        m = merged[:, t, CH * c:CH * c + CH]
                        g.tensor_tensor(m, m, gates[:, 1, t, CH * c:CH * c + CH], ALU.add).then_inc(y.madd, 1)
                if i == 1:
                    g.wait_ge(y.ev_vec, 12)
                    g.dma_start(rw[:], router_w[0].rearrange("(k p) e -> p k e", p=P)).then_inc(rw_in, 16)
                    g.dma_start(rb[:], router_b[0].partition_broadcast(P)).then_inc(rw_in, 16)
                power(y.n2, 2)
                g.wait_ge(y.n2.hn, y.n2.g + 4)
                load_gain(ple_norm[i])
                g.wait_ge(y.ev_vec, 12)
                g.dma_start(pnat[:], p[i, 0].rearrange("(t p) c -> p t c", p=P)).then_inc(p_in, 16)
                power(y.n3, 2)
                g.wait_ge(y.n3.hn, y.n3.g + 4)
                load_gain(attn_norm[1] if i == 0 else final_norm)
                for c in range(2):
                    for t in range(T):
                        g.wait_ge(y.pev_vec, 2 * c + t + 1)
                        m = xs[:, t, CH * c:CH * c + CH]
                        g.tensor_tensor(m, m, psg[:, t, CH * c:CH * c + CH], ALU.add).then_inc(y.padd, 1)
            power(nfin, 2)

        @block.scalar
        def _(a):
            cur = [0]

            def split_to(n, dyn=0, de=0, kinds=None):
                while cur[0] < n:
                    u = cur[0]
                    s = u // 2
                    a.wait_ge(raw_in[s % RAW], 16 * (s // RAW + 1) + de)
                    a.wait_ge(used, dyn + u + 1)
                    src, dst = unit_views(u, raw, hi)
                    a.activation(dst, src, ACT.Copy).then_inc(hi_done, 1)
                    cur[0] += 1

            def norm_square(n, pairs, ready):
                for j, (src, junk) in enumerate(pairs):
                    if ready:
                        a.wait_ge(ready[0], ready[1][j])
                    a.activation(junk, src, ACT.Square, accum_out=ss[:, j:j + 1]).then_inc(n.sq, 1)

            def round_groups(trs, his, dsts, banks, base=0):
                for j, (dst, bank) in enumerate(zip(dsts, banks)):
                    a.wait_ge(trs, base + j + 1)
                    a.activation(dst, bank, ACT.Copy).then_inc(his, 1)

            def x_pairs():
                return [(xs[:, t, CH * h:CH * h + CH], hnat[:, t, CH * h:CH * h + CH]) for t, h in groups]

            def done(u, dyn=0):
                a.wait_ge(used, dyn + u + 1 + US0)

            def attn(i, ready, dyn=0, de=0):
                y, b = layers[i], LBASE[i]
                kw = dict(dyn=dyn, de=de)
                if i:
                    split_to(b + 4, **kw)
                norm_square(y.n1, x_pairs(), ready)
                split_to(b + 4, **kw)
                round_groups(y.n1.tr, y.n1.hi, *hT_groups(hT_hi), y.n1.g)
                if i == 0:
                    a.wait_ge(trig_ok, 1)
                    a.activation(sin[:], ang[:], ACT.Sin).then_inc(ang_ok, 1)
                    a.activation(sh[:], ang[:], ACT.Sin, scale=0.5).then_inc(ang_ok, 1)
                split_to(b + U_L0 + 7, **kw)
                done(b + U_L0 + 3)
                for t in range(T):
                    a.activation(lat[:, t, 0:CH], ps[:, t, :], ACT.Copy).then_inc(y.ev_act, 1)
                split_to(b + U_L1 + 5, **kw)
                done(b + U_L1 + 1)
                for t in range(T):
                    a.activation(lat[:, t, CH:LAT + ROPE], ps[:, 2 + t, 0:160], ACT.Copy).then_inc(y.ev_act, 1)
                a.wait_ge(y.ev_act, 4)
                norm_square(y.nl, lat_pairs(), None)
                for j in range(3):
                    if j == 1:
                        round_groups(y.nl.tr, y.nl.hi, *lat_groups(latT_hi), y.nl.g)
                    u = b + U_V + 4 * j
                    split_to(u + 7, **kw)
                    done(u + 3)
                    for t in range(T):
                        a.activation(vd[:, t, CH * j:CH * j + CH], ps[:, 2 * (j % 2) + t, :], ACT.Copy).then_inc(y.ev_act, 1)
                for c in range(2):
                    u = b + U_UQ + 2 * c
                    split_to(u + 5, **kw)
                    done(u + 1)
                    for t in range(T):
                        a.activation(qnat[:, t, 4 * c:4 * c + 4, :],
                                     ps[:, 2 * ((5 + c) % 2) + t, 0:384].rearrange("p (h d) -> p h d", d=HQK),
                                     ACT.Copy).then_inc(y.ev_act, 1)
                for c in range(2):
                    u = b + U_UKV + c
                    split_to(u + 4, **kw)
                    done(u)
                    for t in range(T):
                        v = ps[:, 2 * ((7 + c) % 2) + t, :].rearrange("p (h d) -> p h d", d=NOPE + VD)
                        a.activation(knat[:, t, 4 * c:4 * c + 4, 0:NOPE], v[:, :, 0:NOPE], ACT.Copy).then_inc(y.ev_act, 1)
                        a.activation(vm[:, t, 4 * c:4 * c + 4, :], v[:, :, NOPE:NOPE + VD], ACT.Copy).then_inc(y.ev_act, 1)
                a.wait_ge(y.rope_k, 1)
                for j in range(6):
                    u = b + U_Q + 4 * j
                    split_to(u + 7, **kw)
                    done(u + 3)
                    if j >= 2:
                        a.wait_ge(y.tround, CHUNK_ROUND[j - 2] + 1)
                    for t in range(T):
                        a.activation(chunk[:, j % 2, t, :], ps[:, 2 * ((9 + j) % 2) + t, :], ACT.Copy,
                                     scale=0.125 if j < 3 else 1.0).then_inc(y.ev_act, 1)
                def exps(n):
                    a.wait_ge(y.smax, n + 1)
                    if n >= 2:
                        a.wait_ge(y.oev, n - 1)
                    nh, w = (MLA_BATCHES[n][2], 128 * (MLA_BATCHES[n][0] + 1)) if n < NB_M else (
                        1, 3 * 128 * (DIL_BATCHES[n - NB_M][0] + 1))
                    for h in range(nh):
                        v = pr[:, n % 2, h * w:h * w + w]
                        ins = a.activation(v, v, ACT.Exp, bias=nmax[:, n % 2, h:h + 1],
                                           accum_out=sums[:, n % 2, h:h + 1])
                    ins.then_inc(y.prob, 1)

                def pt_evac(n):
                    a.wait_ge(y.ptr, n + 1)
                    nb = 4 if n < NB_M else 3 * (DIL_BATCHES[n - NB_M][0] + 1)
                    if nb > 4:
                        a.activation(pT[:, n % 2, 4:nb, :], ps[:, 5, 0:P * (nb - 4)].rearrange("p (b q) -> p b q", q=P), ACT.Copy)
                    m = min(nb, 4)
                    a.activation(pT[:, n % 2, 0:m, :], ps[:, 4, 0:P * m].rearrange("p (b q) -> p b q", q=P),
                                 ACT.Copy).then_inc(y.ptev, 1)

                def round_pair(hp):
                    for m, src in enumerate((qT, kT)):
                        a.activation(qk_hi[hp % 2][:, m], pair_of(src, hp), ACT.Copy).then_inc(y.qk_hi, 1)

                a.wait_ge(y.tevac, 10)
                round_pair(0)

                def gate_evac(j, func, sig):
                    for t in range(T):
                        a.activation(gates[:, j // 2, t, CH * (j % 2):CH * (j % 2) + CH], ps[:, GATE_BANKS[t], :], func).then_inc(sig, 1)

                for n in range(NB + 2):
                    if n < NB:
                        exps(n)
                    if 1 <= n <= NB:
                        if n >= 3:
                            a.wait_ge(y.pv, n - 2)
                        pt_evac(n - 1)
                    j = 3 if n == NB_M else GATE_AT.get(n, 0)
                    if j % 4 == 3 and n >= NB_M:
                        done(b + U_G + j)
                        gate_evac(j // 4, ACT.Copy, y.ev_act)
                    if n in GATE_AT:
                        split_to(b + U_G + GATE_AT[n] + 5, **kw)
                    if n in SPLIT_AT:
                        round_pair(SPLIT_AT[n])
                split_to(b + U_G + 18, **kw)
                for k, (dst, b0) in enumerate(((omT_hi, 4), (odT_hi, 0))):
                    a.wait_ge(y.otr, k + 1)
                    a.activation(tok_blocks(dst, 4), pair_blocks(b0), ACT.Copy).then_inc(y.ohi, 1)
                a.wait_ge(y.ev_act, EV_ACT[17])
                for t in range(T):
                    a.activation(gates[:, 0, t, :], gates[:, 0, t, :], ACT.Sigmoid).then_inc(y.gsig, 1)
                split_to(b + U_G + 19, **kw)
                a.activation(gates[:, 1, :, 0:CH], gates[:, 1, :, 0:CH], ACT.Sigmoid).then_inc(y.gsig, 1)
                done(b + U_G + 15)
                gate_evac(3, ACT.Sigmoid, y.gsig)
                split_to(b + U_BD + 8, **kw)
                round_groups(y.mtr, y.mhi, *hT_groups(hT_hi))
                split_to(b + U_FF, **kw)

            def norm2(i, ready):
                y = layers[i]
                norm_square(y.n2, x_pairs(), ready)
                round_groups(y.n2.tr, y.n2.hi, *hT_groups(hT_hi), y.n2.g)

            def ple(i, ready, dyn=0, de=0):
                y, b = layers[i], PLE0[i]
                kw = dict(dyn=dyn, de=de)
                split_to(b + 4, **kw)
                a.wait_ge(y.ptr2, 1)
                a.activation(tok_blocks(peT_hi, 2), pe_blocks(), ACT.Copy).then_inc(y.phi, 1)
                norm_square(y.n3, x_pairs(), ready)
                round_groups(y.n3.tr, y.n3.hi, *hT_groups(hT_hi), y.n3.g)
                for c in range(2):
                    split_to(min(b + 4 * c + 9, b + 10), **kw)
                    done(b + 4 * c + 5, dyn)
                    for t in range(T):
                        a.activation(psg[:, t, CH * c:CH * c + CH], ps[:, 4 + 2 * c + t, :], ACT.Sigmoid).then_inc(y.pev_act, 1)
                split_to(b + 10, **kw)

            attn(0, (x_in, [16] * 4))
            norm2(0, (layers[0].ev_vec, [9, 10, 11, 12]))
            b = FF0[0]

            def f_sigmoid(u, dyn, n):
                a.wait_ge(used, dyn + u + 1 + US0)
                a.activation(f_sig[:], ps[:, 0:2, :], ACT.Sigmoid).then_inc(f_sigd, 1)

            def f_round(n):
                a.wait_ge(f_tr, n)
                a.activation(tok_blocks(faT_hi, 4), pair_blocks(6), ACT.Copy).then_inc(f_hi, 1)

            split_to(b + 7)
            f_sigmoid(b + 3, 0, 0)
            split_to(b + 8)
            with a.Fori(0, NF - 1) as j:
                ub = b + 8
                dj, dr = j * UPF, j * 16
                cur[0] = ub
                split_to(ub + 5, dj, dr)
                f_round(j + 1)
                split_to(ub + 7, dj, dr)
                a.wait_ge(f_actd, j + 1)
                f_sigmoid(ub + 3, dj, 0)
                split_to(ub + 12, dj, dr)
            cur[0] = b + 80
            split_to(b + 84)
            f_round(NF)
            ple(0, (f_xadd, [2 * NF] * 2 + [2 * NF + 1] * 2))
            attn(1, (layers[0].padd, [1, 2, 3, 4]))
            norm2(1, (layers[1].ev_vec, [9, 10, 11, 12]))
            a.activation(hn_hi[:], hnat[:], ACT.Copy).then_inc(hn_h, 1)
            a.wait_ge(r_v, 1)
            a.activation(w12[:, 0, :], dv[:], ACT.Sigmoid).then_inc(r_sg, 1)
            a.activation(w12[:, 1, :], dv[:], ACT.Sigmoid, scale=-1.0).then_inc(r_sg, 1)
            a.wait_ge(r_np, 1)
            npv = a.value_load(npass[0:1, 0:1], min_val=1, max_val=2)
            b = FF0[1]
            with a.Fori(0, npv) as q:
                dq = q * (UPE * NE)
                rq = q * (16 * 7 * NE)

                def gather_round(ex):
                    a.wait_ge(e_gath, ex + 1)
                    a.activation(hs_hi[:], ps[:, 6:8, :].rearrange("p b (k s) -> p (b k) s", s=P),
                                 ACT.Copy).then_inc(e_hsh, 1)

                def step(ub, dyn, dr, ch, ex, first=False, sel_t=False, ysc=(), gath=None):
                    cur[0] = ub
                    if 1 in ysc:
                        split_to(ub + 3, dyn, dr)
                        y_round(1, ub - 1, dyn, ex)
                    split_to(ub + 5, dyn, dr)
                    a.wait_ge(e_tr, ch)
                    a.activation(eaT_hi[:], ps[:, 6, :].rearrange("p (k s) -> p k s", s=P), ACT.Copy).then_inc(e_hi, 1)
                    split_to(ub + 7, dyn, dr)
                    a.wait_ge(e_actd, ch + 1)
                    done(ub + 3, dyn)
                    a.activation(e_sig[:], ps[:, 0, :], ACT.Sigmoid).then_inc(e_sigd, 1)
                    split_to(ub + 10, dyn, dr)
                    if sel_t:
                        a.wait_ge(e_st, ex + 1)
                        a.activation(selT[:], ps[:, 7, 0:S], ACT.Copy)
                        a.activation(gslot[:], ps[:, 7, S:S + 1], ACT.Copy).then_inc(e_stev, 1)
                    if 0 in ysc:
                        y_round(0, ub + 5, dyn, ex)
                    split_to(ub + 12, dyn, dr)
                    if gath is not None:
                        gather_round(gath)

                def y_round(c, u, dyn, ex):
                    done(u, dyn)
                    a.wait_ge(e_stev, ex + 1)
                    a.activation(y_hi[:, CH * c:CH * c + CH], ps[:, 4 + c, :], ACT.Copy, scale=gslot[:, 0:1]).then_inc(e_yhi, 1)

                gather_round(q * NE)
                cur[0] = b
                split_to(b + 7, dq, rq)
                done(b + 3, dq)
                a.wait_ge(e_actd, q * (NF * NE) + 1)
                a.activation(e_sig[:], ps[:, 0, :], ACT.Sigmoid).then_inc(e_sigd, 1)
                split_to(b + 8, dq, rq)
                step(b + 8, dq, rq, q * (NF * NE) + 1, q * NE)
                with a.Fori(0, NE - 1) as e:
                    dyn = e * UPE + dq
                    dr = e * 112 + rq
                    ch0 = q * (NF * NE) + e * NF
                    ex = q * NE + e
                    for f in range(2, NF):
                        step(b + 20 + 12 * (f - 2), dyn, dr, ch0 + f, ex, sel_t=(f == 2),
                             gath=(ex + 1) if f == NF - 1 else None)
                    step(b + 80, dyn, dr, ch0 + NF, ex, ysc=(0,))
                    step(b + 92, dyn, dr, ch0 + NF + 1, ex, ysc=(1,))
                bl = b + UPE * (NE - 1)
                el = NE - 1
                for f in range(2, NF):
                    step(bl + 20 + 12 * (f - 2), dq, rq, q * (NF * NE) + (el * NF + f), q * NE + el, sel_t=(f == 2))
                cur[0] = bl + 80
                split_to(bl + 84, dq, rq)
                a.wait_ge(e_tr, q * (NF * NE) + NE * NF)
                a.activation(eaT_hi[:], ps[:, 6, :].rearrange("p (k s) -> p k s", s=P), ACT.Copy).then_inc(e_hi, 1)
                y_round(0, bl + 81, dq, q * NE + el)
                y_round(1, bl + 83, dq, q * NE + el)
            dyn, de = (npv - 1) * (UPE * NE), (npv - 1) * (16 * 7 * NE)
            added = npv * (2 * NE) + 2
            ple(1, (e_xadd, [added] * 4), dyn, de)
            norm_square(nfin, x_pairs(), (layers[1].padd, [1, 2, 3, 4]))

        @block.vector
        def _(v):
            cur = [0]
            vl = [0]

            def link(ins):
                vl[0] += 1
                ins.then_inc(v_link, 1)
                v.wait_ge(v_link, vl[0])

            def split_to(n, dyn=0):
                while cur[0] < n:
                    u = cur[0]
                    v.wait_ge(hi_done, dyn + u + 1)
                    src, h = unit_views(u, raw, hi)
                    _, dst = unit_views(u, raw, lo)
                    v.tensor_tensor(dst, src, h, ALU.subtract).then_inc(lo_done, 1)
                    cur[0] += 1

            def done(u, dyn=0):
                v.wait_ge(used, dyn + u + 1 + US0)

            def norm_scale(n, inv_n, pieces, ngain, gsem):
                if len(inv_n) == 1:
                    v.wait_ge(n.sq, n.g + 2)
                    link(v.tensor_scalar(part[:], ss[:, 0:2], 1.0 / inv_n[0][1], EPS, ALU.mult, ALU.add))
                    v.wait_ge(n.sq, n.g + 4)
                    ins = v.scalar_tensor_tensor(out=ms[:, 0:2], in0=ss[:, 2:4], scalar=1.0 / inv_n[0][1], in1=part[:],
                                                 op0=ALU.mult, op1=ALU.add)
                else:
                    v.wait_ge(n.sq, n.g + 4)
                    for c, k in inv_n:
                        ins = v.tensor_scalar(ms[:, c:c + 2], ss[:, c:c + 2], 1.0 / k, EPS, ALU.mult, ALU.add)
                ins.then_inc(n.ms, 1)
                v.wait_ge(n.rs, n.k + 1)
                v.wait_ge(gsem, ngain)
                for src, c, gv, dst in pieces:
                    v.scalar_tensor_tensor(out=dst, in0=src, scalar=rstd[:, c:c + 1], in1=gv,
                                           op0=ALU.mult, op1=ALU.mult).then_inc(n.hn, 1)

            def x_norm(n, ngain):
                norm_scale(n, [(0, D)], [(xs[:, t, CH * h:CH * h + CH], t, gain[:, CH * h:CH * h + CH], hnat[:, t, CH * h:CH * h + CH])
                                             for t, h in groups],
                           16 * max(ngain - 1, 1), gain_in if ngain > 1 else gain0_in)

            def rest_groups(his, los, hi_d, lo_d, banks, base=0):
                for j, (h, l, bank) in enumerate(zip(hi_d, lo_d, banks)):
                    v.wait_ge(his, base + j + 1)
                    v.tensor_tensor(l, bank, h, ALU.subtract).then_inc(los, 1)

            def hT_rest(n):
                rest_groups(n.hi, n.lo, hT_groups(hT_hi)[0], *hT_groups(hT_lo), n.g)

            def tables():
                v.wait_ge(const_ok, 2)
                link(v.tensor_copy(dflt[:], dint[:]))
                v.tensor_copy(dist[:, 0, :], dflt[:])
                for m, dil in ((1, 4), (2, 16)):
                    link(v.tensor_scalar(dand[:], dint[:], dil - 1, None, ALU.bitwise_and))
                    link(v.tensor_copy(dmod[:], dand[:]))
                    link(v.tensor_scalar(dmod[:], dmod[:], 1.0, BIG, ALU.min, ALU.mult))
                    link(v.tensor_tensor(dist[:, m, :], dflt[:], dmod[:], ALU.add))
                v.wait_ge(pos_in, 16)
                link(v.tensor_copy(posf[:], posi[:]))
                for t in range(T):
                    ins = v.tensor_scalar(ang[:, t, :], freq[:], posf[:, t:t + 1], None, ALU.mult)
                link(ins)
                magic = 1.5 * 2.0 ** 23
                link(v.tensor_scalar(kq[:], ang[:], 1.0 / (2 * np.pi), magic, ALU.mult, ALU.add))
                link(v.tensor_scalar(kq[:], kq[:], -magic, None, ALU.add))
                rest = 2 * np.pi
                for bits in (5, 13, 21, None):
                    part = float(np.float32(rest)) if bits is None else float(np.floor(rest * 2.0 ** bits) / 2.0 ** bits)
                    rest -= part
                    link(v.scalar_tensor_tensor(out=ang[:], in0=kq[:], scalar=-part, in1=ang[:], op0=ALU.mult, op1=ALU.add))
                link(v.tensor_scalar(ang[:], ang[:], 3.1415925, -3.1415925, ALU.min, ALU.max))
                v.sem_inc(trig_ok, 1)

            def rotary():
                v.wait_ge(ang_ok, 2)
                link(v.tensor_tensor(sh[:], sh[:], sh[:], ALU.mult))
                v.tensor_scalar(cos[:], sh[:], -2.0, 1.0, ALU.mult, ALU.add).then_inc(rot_ok, 1)

            def attn(i, dyn=0):
                y, b = layers[i], LBASE[i]
                if i:
                    split_to(b + 4, dyn)
                x_norm(y.n1, 1 + 3 * i)
                split_to(b + 4, dyn)
                hT_rest(y.n1)
                if i == 0:
                    tables()
                split_to(b + U_L1 + 5, dyn)
                if i == 0:
                    rotary()
                norm_scale(y.nl, [(0, QR), (2, KVR)],
                           [(lat[:, t, 0:QR], t, glat[:, 0:QR], lat[:, t, 0:QR]) for t in range(T)]
                           + [(lat[:, t, QR:LAT], 2 + t, glat[:, QR:LAT], lat[:, t, QR:LAT]) for t in range(T)],
                           32 * (i + 1), glat_in)
                split_to(b + U_V + 7, dyn)
                rest_groups(y.nl.hi, y.nl.lo, lat_groups(latT_hi)[0], *lat_groups(latT_lo), y.nl.g)
                r = 0
                for j in range(6):
                    split_to(b + U_Q + 4 * j + 7, dyn)
                    for dst, rr in ROUNDS_AFTER[j]:
                        v.wait_ge(y.tround, r + 1)
                        b0 = 4 + 2 * (r % 2)
                        if dst == "qk":
                            d = qT[:, 4 * rr:4 * rr + 4, :] if rr < 3 else kT[:, 4 * (rr - 3):4 * (rr - 3) + 4, :]
                            v.tensor_copy(d.rearrange("p k (t j) -> p t k j", t=T), pair_blocks(b0)).then_inc(y.tevac, 1)
                        else:
                            d = (qmT if dst == "mq" else kmT)[0:HQK, 4 * rr:4 * rr + 4, :]
                            v.tensor_copy(d.rearrange("p k (t j) -> p t k j", t=T), pair_blocks(b0, HQK)).then_inc(y.tevac, 1)
                        r += 1
                assert r == 10

                def prep(n):
                    v.wait_ge(y.score, n + 1)
                    if n >= 2:
                        v.wait_ge(y.ptr, n - 1)
                    b0 = n % 2
                    if n < NB_M:
                        t, h0, nh = MLA_BATCHES[n]
                        nk = P * (t + 1)
                        m = cmask[:, 256 - nk:256].unsqueeze(1).to_broadcast([P, nh, nk])
                        w = pr[:, n % 2, 0:CH].rearrange("p (h k) -> p h k", h=nh)
                        link(v.scalar_tensor_tensor(out=w, in0=ps[:, b0, :].rearrange("p (h k) -> p h k", h=nh),
                                                    scalar=float(HQK) ** -0.5, in1=m, op0=ALU.mult, op1=ALU.add))
                        v.tensor_reduce(nmax[:, n % 2, 0:nh], w, AX.X, ALU.max, negate=True).then_inc(y.smax, 1)
                    else:
                        t, h = DIL_BATCHES[n - NB_M]
                        nk = P * (t + 1)
                        for m in range(DG):
                            sc = ps[:, b0 + (nk * m) // CH, (nk * m) % CH:(nk * m) % CH + nk]
                            ins = v.scalar_tensor_tensor(out=pr[:, n % 2, nk * m:nk * m + nk],
                                                         in0=dist[:, m, 256 - nk:256], scalar=-SLOPES[m * DH + h],
                                                         in1=sc, op0=ALU.mult, op1=ALU.add)
                        link(ins)
                        v.tensor_reduce(nmax[:, n % 2, 0:1], pr[:, n % 2, 0:3 * nk], AX.X, ALU.max,
                                        negate=True).then_inc(y.smax, 1)

                def normalise(n):
                    v.wait_ge(y.pv, n + 1)
                    o = ps[:, 6, :]
                    if n < NB_M:
                        t, h0, nh = MLA_BATCHES[n]
                        dst = o_mla[:, t, h0 * 64:(h0 + nh) * 64]
                    else:
                        (t, h0), nh = DIL_BATCHES[n - NB_M], 1
                        dst = o_dil[:, t, h0 * 64:(h0 + nh) * 64]
                    link(v.reciprocal(rsum[:, n % 2, 0:nh], sums[:, n % 2, 0:nh]))
                    v.tensor_tensor(dst.rearrange("p (h d) -> p h d", d=64),
                                    o[:, 0:64 * nh].rearrange("p (h d) -> p h d", d=64),
                                    rsum[:, n % 2, 0:nh].unsqueeze(2).to_broadcast([P, nh, 64]),
                                    ALU.mult).then_inc(y.oev, 1)

                def rest_pair(hp):
                    for m, (src, dst) in enumerate(((qT, qT_lo), (kT, kT_lo))):
                        v.wait_ge(y.qk_hi, 2 * hp + m + 1)
                        v.tensor_tensor(pair_of(dst, hp), pair_of(src, hp), qk_hi[hp % 2][:, m],
                                        ALU.subtract).then_inc(y.qk_lo, 1)

                for n in range(NB + 2):
                    if n < NB:
                        prep(n)
                    if n >= 2:
                        normalise(n - 2)
                    if n == 1:
                        rest_pair(0)
                    if n - 1 in SPLIT_AT:
                        rest_pair(SPLIT_AT[n - 1])
                    if n - 1 in GATE_AT:
                        split_to(b + U_G + GATE_AT[n - 1] + 5, dyn)
                split_to(b + U_G + 17, dyn)
                for k, (h, l, b0) in enumerate(((omT_hi, omT_lo, 4), (odT_hi, odT_lo, 0))):
                    v.wait_ge(y.ohi, k + 1)
                    v.tensor_tensor(tok_blocks(l, 4), pair_blocks(b0), tok_blocks(h, 4), ALU.subtract).then_inc(y.olo, 1)
                for n, u in enumerate((U_BM, U_BM + 2, U_BD, U_BD + 2)):
                    split_to(b + u + 5, dyn)
                    done(b + u + 1)
                    c = n % 2
                    v.wait_ge(y.gsig, (2, 2, 3, 5)[n])
                    for t in range(T):
                        gv = gates[:, n // 2, t, CH * c:CH * c + CH]
                        dst = merged[:, t, CH * c:CH * c + CH] if n < 2 else gv
                        v.tensor_tensor(dst, gv, ps[:, BRANCH_BANKS[n % 2][t], :], ALU.mult).then_inc(y.ev_vec, 1)
                rest_groups(y.mhi, y.mlo, hT_groups(hT_hi)[0], *hT_groups(hT_lo))
                for c in range(2):
                    split_to(min(b + U_O + 4 * c + 7, b + U_FF), dyn)
                    done(b + U_O + 4 * c + 3)
                    for t in range(T):
                        m = xs[:, t, CH * c:CH * c + CH]
                        v.tensor_tensor(m, m, ps[:, 2 * ((23 + c) % 2) + t, :], ALU.add).then_inc(y.ev_vec, 1)

            def ple(i, dyn=0):
                y, b = layers[i], PLE0[i]
                split_to(b + 4, dyn)
                v.wait_ge(y.phi, 1)
                v.tensor_tensor(tok_blocks(peT_lo, 2), pe_blocks(), tok_blocks(peT_hi, 2), ALU.subtract).then_inc(y.plo, 1)
                x_norm(y.n3, 3 + 3 * i)
                hT_rest(y.n3)
                split_to(b + 10, dyn)
                for c in range(2):
                    v.wait_ge(y.pev_act, 2 * c + 2)
                    for t in range(T):
                        m = psg[:, t, CH * c:CH * c + CH]
                        v.tensor_tensor(m, m, ps[:, 2 * c + t, :], ALU.mult).then_inc(y.pev_vec, 1)

            attn(0)
            x_norm(layers[0].n2, 2)
            hT_rest(layers[0].n2)
            b = FF0[0]

            def f_gate():
                v.tensor_tensor(f_sig[:], f_sig[:], ps[:, 0:2, :], ALU.mult).then_inc(f_t1, 1)

            def f_up():
                v.tensor_tensor(f_act[:], f_sig[:], ps[:, 2:4, :], ALU.mult).then_inc(f_actd, 1)

            def f_rest():
                v.tensor_tensor(tok_blocks(faT_lo, 4), pair_blocks(6), tok_blocks(faT_hi, 4), ALU.subtract).then_inc(f_lo, 1)

            def f_add(c):
                m = xs[:, :, CH * c:CH * c + CH]
                v.tensor_tensor(m, m, ps[:, 4:6, :], ALU.add).then_inc(f_xadd, 1)

            split_to(b + 8)
            v.wait_ge(f_sigd, 1)
            f_gate()
            done(b + 7)
            v.wait_ge(f_t1, 1)
            f_up()

            def f_step(ub, dj, n, first):
                cur[0] = ub
                split_to(ub + 3, dj)
                if not first:
                    done(ub - 1, dj)
                    f_add(1)
                split_to(ub + 5, dj)
                v.wait_ge(f_hi, n)
                f_rest()
                split_to(ub + 8, dj)
                v.wait_ge(f_sigd, n + 1)
                f_gate()
                split_to(ub + 9, dj)
                done(ub + 5, dj)
                f_add(0)
                split_to(ub + 12, dj)
                done(ub + 9, dj)
                v.wait_ge(f_t1, n + 1)
                f_up()

            f_step(b + 8, 0, 1, True)
            with v.Fori(0, NF - 2) as j:
                f_step(b + 20, j * UPF, j + 2, False)
            cur[0] = b + 80
            split_to(b + 84)
            done(b + 79)
            f_add(1)
            v.wait_ge(f_hi, NF)
            f_rest()
            done(b + 81)
            f_add(0)
            done(b + 83)
            f_add(1)
            ple(0)
            attn(1)
            y = layers[1]
            x_norm(y.n2, 5)
            hT_rest(y.n2)
            v.wait_ge(rw_in, 32)
            link(v.tensor_copy(rw_hi[:], rw[:]))
            v.tensor_tensor(rw_lo[:], rw[:], rw_hi[:], ALU.subtract).then_inc(r_w, 1)
            v.wait_ge(hn_h, 1)
            v.tensor_tensor(hn_lo[:], hnat[:], hn_hi[:], ALU.subtract).then_inc(hn_l, 1)
            v.wait_ge(r_log, 1)
            link(v.tensor_tensor(lg[:], ps[:, 0, 0:2 * NE].rearrange("p (t e) -> p t e", e=NE),
                                 rb[:].unsqueeze(1).to_broadcast([P, T, NE]), ALU.add))
            for t in range(T):
                link(v.max(out=mx8[:, t, :], in_=lg[:, t, :]))
                link(v.max_index(ix8[:, t, :], mx8[:, t, :], lg[:, t, :]))
            v.tensor_tensor(dv[:], mx8[:, :, 0], mx8[:, :, 1], ALU.subtract).then_inc(r_v, 1)
            link(v.tensor_copy(ixf[:], ix8[:]))
            for t in range(T):
                v.tensor_scalar(oh1[:, t, :], iota[:, 0:NE], ixf[:, t, 0:1], None, ALU.is_equal)
                link(v.tensor_scalar(oh2[:, t, :], iota[:, 0:NE], ixf[:, t, 1:2], None, ALU.is_equal))
            v.tensor_tensor(mask[:], oh1[:], oh2[:], ALU.add).then_inc(r_msk, 1)
            v.wait_ge(r_sg, 2)
            for t in range(T):
                link(v.tensor_scalar(gts[:, t, :], oh1[:, t, :], w12[:, 0, t:t + 1], None, ALU.mult))
                v.scalar_tensor_tensor(out=gts[:, t, :], in0=oh2[:, t, :], scalar=w12[:, 1, t:t + 1],
                                       in1=gts[:, t, :], op0=ALU.mult, op1=ALU.add)
            v.wait_ge(r_rank, 1)
            link(v.scalar_tensor_tensor(out=slot[:], in0=ps[:, 1, 0:2 * NE].rearrange("p (t e) -> p t e", e=NE),
                                        scalar=1.0, in1=mask[:], op0=ALU.add, op1=ALU.mult))
            link(v.tensor_scalar(slot[:], slot[:], -1.0, None, ALU.add))
            link(v.tensor_reduce(tot[:], ps[:, 1, 2 * NE:3 * NE], AX.X, ALU.max))
            v.tensor_scalar(npass[:], tot[0:1, :], float(P), 1.0, ALU.is_gt, ALU.add).then_inc(r_np, 1)
            v.wait_ge(r_np, 1)
            npv = v.value_load(npass[0:1, 0:1], min_val=1, max_val=2)
            b = FF0[1]
            with v.Fori(0, npv) as q:
                dq = q * (UPE * NE)

                def build(e):
                    for t in range(T):
                        v.tensor_scalar(sel[:, t, :], iota[:], slot[:, t, bass.ds(e, 1)], None, ALU.is_equal)
                    v.tensor_copy(gcol[:].unsqueeze(2), gts[:, :, bass.ds(e, 1)]).then_inc(e_sel, 1)

                def gather_copy(ex):
                    v.wait_ge(e_gath, ex + 1)
                    v.tensor_copy(hs_lo[:].rearrange("p (b k) s -> p b k s", b=2),
                                  ps[:, 2:4, :].rearrange("p b (k s) -> p b k s", s=P)).then_inc(e_hsl, 1)

                def y_rest(c, ex):
                    v.wait_ge(e_yhi, ex * 2 + (c + 1))
                    v.scalar_tensor_tensor(out=y_lo[:, CH * c:CH * c + CH], in0=ps[:, 4 + c, :], scalar=gslot[:, 0:1],
                                           in1=y_hi[:, CH * c:CH * c + CH], op0=ALU.mult, op1=ALU.subtract).then_inc(e_ylo, 1)

                def x_add(ex):
                    v.wait_ge(e_scat, ex + 1)
                    for t, banks in ((0, ps[:, 2:4, :]), (1, ps[:, 6:8, :])):
                        m = xs[:, t, :].rearrange("p (c n) -> p c n", c=2)
                        v.tensor_tensor(m, m, banks, ALU.add).then_inc(e_xadd, 1)

                def gate_up(ch):
                    v.wait_ge(e_sigd, ch + 1)
                    v.tensor_tensor(e_sig[:], e_sig[:], ps[:, 0, :], ALU.mult).then_inc(e_t1, 1)

                def up(ch, u, dyn):
                    done(u, dyn)
                    v.wait_ge(e_t1, ch + 2)
                    v.tensor_tensor(e_act[:], e_sig[:], ps[:, 1, :], ALU.mult).then_inc(e_actd, 1)

                def step(ub, dyn, ch, ex, ysc=(), scat=False, sel_next=None, gath=None):
                    cur[0] = ub
                    if 1 in ysc:
                        split_to(ub + 3, dyn)
                        y_rest(1, ex)
                    split_to(ub + 5, dyn)
                    v.wait_ge(e_hi, ch)
                    v.tensor_tensor(eaT_lo[:], ps[:, 6, :].rearrange("p (k s) -> p k s", s=P), eaT_hi[:],
                                    ALU.subtract).then_inc(e_lo, 1)
                    split_to(ub + 8, dyn)
                    gate_up(ch)
                    split_to(ub + 10, dyn)
                    if 0 in ysc:
                        y_rest(0, ex)
                    if scat:
                        x_add(ex)
                    if sel_next is not None:
                        v.wait_ge(e_st, ex + 1)
                        build(sel_next)
                    split_to(ub + 12, dyn)
                    up(ch, ub + 9, dyn)
                    if gath is not None:
                        gather_copy(gath)

                build(0)
                gather_copy(q * NE)
                cur[0] = b
                split_to(b + 8, dq)
                ch = q * (NF * NE)
                gate_up(ch)
                up(ch, b + 7, dq)
                step(b + 8, dq, ch + 1, q * NE)
                with v.Fori(0, NE - 1) as e:
                    dyn = e * UPE + dq
                    ch0 = q * (NF * NE) + e * NF
                    ex = q * NE + e
                    for f in range(2, NF):
                        step(b + 20 + 12 * (f - 2), dyn, ch0 + f, ex, sel_next=(e + 1) if f == 4 else None,
                             gath=(ex + 1) if f == NF - 1 else None)
                    step(b + 80, dyn, ch0 + NF, ex, ysc=(0,))
                    step(b + 92, dyn, ch0 + NF + 1, ex, ysc=(1,), scat=True)
                bl = b + UPE * (NE - 1)
                el = NE - 1
                for f in range(2, NF):
                    step(bl + 20 + 12 * (f - 2), dq, q * (NF * NE) + (el * NF + f), q * NE + el)
                cur[0] = bl + 80
                split_to(bl + 84, dq)
                v.wait_ge(e_hi, q * (NF * NE) + NE * NF)
                v.tensor_tensor(eaT_lo[:], ps[:, 6, :].rearrange("p (k s) -> p k s", s=P), eaT_hi[:],
                                ALU.subtract).then_inc(e_lo, 1)
                y_rest(0, q * NE + el)
                y_rest(1, q * NE + el)
                x_add(q * NE + el)
                v.tensor_scalar(slot[:], slot[:], -float(P), None, ALU.add).then_inc(r_msk, 1)
                v.wait_ge(r_msk, q + 2)
            ple(1, (npv - 1) * (UPE * NE))
            x_norm(nfin, 7)

        @block.tensor
        def _(pe):
            def unit(u, dyn, l_hi, l_lo, dims, k0, outs, c0, first, last):
                nk, w = dims
                pe.wait_ge(lo_done, dyn + u + 1 + LO0)
                wh = hi[:, u % RING, 0:nk * w].rearrange("p (k n) -> p k n", k=nk)
                wl = lo[:, u % RING, 0:nk * w].rearrange("p (k n) -> p k n", k=nk)
                for kk in range(nk):
                    for t, bank in enumerate(outs):
                        o = ps[:, bank, c0:c0 + w]
                        ah, al = l_hi[:, k0 + kk, P * t:P * t + P], l_lo[:, k0 + kk, P * t:P * t + P]
                        pe.matmul(o, ah, wh[:, kk, :], start=(first and kk == 0), stop=False)
                        pe.matmul(o, ah, wl[:, kk, :], start=False, stop=False)
                        ins = pe.matmul(o, al, wh[:, kk, :], start=False, stop=(last and kk == nk - 1))
                ins.then_inc(used, 1)

            def cols(u, dyn, l_hi, l_lo, outs, w=CH, nku=2, units=4, ready=None):
                for h in range(units):
                    if ready and h % 2 == 0:
                        pe.wait_ge(ready[0], ready[1] + 2 + h)
                    unit(u + h, dyn, l_hi, l_lo, (nku, w), nku * h, outs, 0, h == 0, h == units - 1)

            def turn_tiles(src, trs, ready, base):
                for j, (t, h) in enumerate(groups):
                    pe.wait_ge(ready, base + j + 1)
                    for k in range(4):
                        ins = pe.transpose(ps[:, 4 + j, P * k:P * k + P], src[:, t, CH * h + P * k:CH * h + P * k + P], ident[:])
                    ins.then_inc(trs, 1)

            def x_turn(n):
                turn_tiles(hnat, n.tr, n.hn, n.g)

            def attn(i, dyn=0):
                y, b = layers[i], LBASE[i]
                x_turn(y.n1)
                if i:
                    pe.wait_ge(layers[0].pev_vec, 4)
                cols(b + U_L0, dyn, hT_hi, hT_lo, (0, 1), ready=(y.n1.lo, y.n1.g))
                cols(b + U_L1, dyn, hT_hi, hT_lo, (2, 3), w=160, nku=4, units=2)

                def evacuated(n):
                    pe.wait_ge(y.ev_act, EV_ACT[n])

                for j in range(3):
                    evacuated(j)
                    cols(b + U_V + 4 * j, dyn, hT_hi, hT_lo, (2 * (j % 2), 2 * (j % 2) + 1))
                    if j == 0:
                        for t in range(T):
                            pe.wait_ge(y.nl.hn, y.nl.g + 4)
                            for k in range(KQ):
                                ins = pe.transpose(ps[:, 4 + 2 * t, P * k:P * k + P], lat[:, t, P * k:P * k + P], ident[:])
                            ins.then_inc(y.nl.tr, 1)
                            for k in range(KKV):
                                ins = pe.transpose(ps[:, 5 + 2 * t, P * k:P * k + P], lat[:, t, QR + P * k:QR + P * k + P], ident[:])
                            ins.then_inc(y.nl.tr, 1)
                pe.wait_ge(y.nl.lo, y.nl.g + 4)
                for c in range(2):
                    n = 5 + c
                    evacuated(n - 2)
                    for h in range(2):
                        unit(b + U_UQ + 2 * c + h, dyn, latT_hi, latT_lo, (KQ, 192), 0,
                             (2 * (n % 2), 2 * (n % 2) + 1), 192 * h, True, True)
                for c in range(2):
                    n = 7 + c
                    evacuated(n - 2)
                    unit(b + U_UKV + c, dyn, latT_hi, latT_lo, (KKV, CH), KQ, (2 * (n % 2), 2 * (n % 2) + 1), 0, True, True)
                r = 0
                for j in range(6):
                    n = 9 + j
                    evacuated(n - 2)
                    cols(b + U_Q + 4 * j, dyn, hT_hi, hT_lo, (2 * (n % 2), 2 * (n % 2) + 1))
                    for dst, rr in ROUNDS_AFTER[j]:
                        if r >= 2:
                            pe.wait_ge(y.tevac, r - 1)
                        if dst == "qk":
                            evacuated(9 + rr)
                            src = [[chunk[:, rr % 2, t, P * k:P * k + P] for k in range(4)] for t in range(T)]
                        elif dst == "mq":
                            pe.wait_ge(y.rope_q, 1)
                            src = [[qnat[:, t, 4 * rr + k, :] for k in range(4)] for t in range(T)]
                        else:
                            evacuated(8)
                            pe.wait_ge(y.rope_k, 1)
                            src = [[knat[:, t, 4 * rr + k, :] for k in range(4)] for t in range(T)]
                        m = P if dst == "qk" else HQK
                        for t in range(T):
                            for k in range(4):
                                ins = pe.transpose(ps[0:m, 4 + 2 * (r % 2) + t, P * k:P * k + P], src[t][k], ident[:])
                        ins.then_inc(y.tround, 1)
                        r += 1

                def scores(n):
                    if n >= 2:
                        pe.wait_ge(y.smax, n - 1)
                    b0 = n % 2
                    if n < NB_M:
                        t, h0, nh = MLA_BATCHES[n]
                        nk = P * (t + 1)
                        for h in range(nh):
                            ins = pe.matmul(ps[:, b0, nk * h:nk * h + nk], qmT[0:HQK, h0 + h, P * t:P * t + P],
                                            kmT[0:HQK, h0 + h, 0:nk], start=True, stop=True)
                    else:
                        t, h = DIL_BATCHES[n - NB_M]
                        nk = P * (t + 1)
                        r0, blk = 64 * (h % 2), h // 2
                        q_hi, k_hi = qk_hi[blk % 2][:, 0], qk_hi[blk % 2][:, 1]
                        pe.wait_ge(y.qk_lo, 2 * blk + 2)
                        for m in range(DG):
                            o = ps[:, b0 + (nk * m) // CH, (nk * m) % CH:(nk * m) % CH + nk]
                            qh, kh = q_hi[r0:r0 + 64, m, P * t:P * t + P], k_hi[r0:r0 + 64, m, 0:nk]
                            pe.matmul(o, qh, kh, start=True, stop=False)
                            pe.matmul(o, qh, kT_lo[r0:r0 + 64, 4 * m + blk, 0:nk], start=False, stop=False)
                            ins = pe.matmul(o, qT_lo[r0:r0 + 64, 4 * m + blk, P * t:P * t + P], kh, start=False, stop=True)
                    ins.then_inc(y.score, 1)

                def turn_probs(n):
                    pe.wait_ge(y.prob, n + 1)
                    if n >= 1:
                        pe.wait_ge(y.ptev, n)
                    nb = 4 if n < NB_M else 3 * (DIL_BATCHES[n - NB_M][0] + 1)
                    for k in range(nb):
                        ins = pe.transpose(ps[:, 4 + k // 4, P * (k % 4):P * (k % 4) + P], pr[:, n % 2, P * k:P * k + P], ident[:])
                    ins.then_inc(y.ptr, 1)

                def values(n):
                    pe.wait_ge(y.ptev, n + 1)
                    if n >= 1:
                        pe.wait_ge(y.oev, n)
                    if n < NB_M:
                        t, h0, nh = MLA_BATCHES[n]
                        for h in range(nh):
                            for k in range(t + 1):
                                ins = pe.matmul(ps[:, 6, 64 * h:64 * h + 64], pT[:, n % 2, (t + 1) * h + k, :],
                                                vm[:, k, h0 + h, :], start=(k == 0), stop=(k == t))
                    else:
                        t, h = DIL_BATCHES[n - NB_M]
                        for m in range(DG):
                            for k in range(t + 1):
                                hd = 64 * (m * DH + h)
                                ins = pe.matmul(ps[:, 6, 0:64], pT[:, n % 2, (t + 1) * m + k, :],
                                                vd[:, k, hd:hd + 64], start=(m == 0 and k == 0),
                                                stop=(m == DG - 1 and k == t))
                    ins.then_inc(y.pv, 1)

                pe.wait_ge(y.tevac, 10)
                evacuated(14)
                def gate_unit(j):
                    if j % 4 == 0 and j:
                        evacuated(14 + j // 4)
                    unit(b + U_G + j, dyn, hT_hi, hT_lo, (2, CH), 2 * (j % 4), GATE_BANKS, 0, j % 4 == 0, j % 4 == 3)

                for n in range(NB + 2):
                    if n < NB:
                        scores(n)
                    if n in GATE_AT:
                        gate_unit(GATE_AT[n])
                    if 1 <= n <= NB:
                        turn_probs(n - 1)
                    if n >= 2:
                        values(n - 2)
                gate_unit(13)
                pe.wait_ge(y.oev, NB)
                pe.wait_ge(y.smax, NB)
                for k, (src, b0) in enumerate(((o_mla, 4), (o_dil, 0))):
                    for t in range(T):
                        for m in range(4):
                            ins = pe.transpose(ps[:, b0 + t, P * m:P * m + P], src[:, t, P * m:P * m + P], ident[:])
                    ins.then_inc(y.otr, 1)
                gate_unit(14)
                gate_unit(15)
                pe.wait_ge(y.olo, 2)
                for k in range(4):
                    if k >= 2:
                        pe.wait_ge(y.ev_vec, 2 * (k - 1))
                    lh, ll = ((omT_hi, omT_lo), (odT_hi, odT_lo))[k // 2]
                    cols(b + U_BM + 2 * k, dyn, lh, ll, BRANCH_BANKS[k % 2], nku=2, units=2)
                turn_tiles(merged, y.mtr, y.madd, 0)
                for c in range(2):
                    pe.wait_ge(y.ev_vec, 6 + 2 * c)
                    n = 23 + c
                    cols(b + U_O + 4 * c, dyn, hT_hi, hT_lo, (2 * (n % 2), 2 * (n % 2) + 1), ready=(y.mlo, 0))

            def ple(i, dyn=0):
                y, b = layers[i], PLE0[i]
                pe.wait_ge(p_in, 16 * (i + 1))
                for t in range(T):
                    for k in range(2):
                        ins = pe.transpose(ps[:, 0, PD * t + P * k:PD * t + P * k + P], pnat[:, t, P * k:P * k + P], ident[:])
                ins.then_inc(y.ptr2, 1)
                pe.wait_ge(y.plo, 1)
                for c in range(2):
                    unit(b + c, dyn, peT_hi, peT_lo, (2, CH), 0, (2 * c, 2 * c + 1), 0, True, True)
                x_turn(y.n3)
                for c in range(2):
                    cols(b + 2 + 4 * c, dyn, hT_hi, hT_lo, (4 + 2 * c, 5 + 2 * c), ready=(y.n3.lo, y.n3.g))

            pe.wait_ge(const_ok, 1)
            attn(0)
            x_turn(layers[0].n2)
            b = FF0[0]
            cols(b, 0, hT_hi, hT_lo, (0, 1), ready=(layers[0].n2.lo, layers[0].n2.g))
            cols(b + 4, 0, hT_hi, hT_lo, (2, 3))

            def f_turn(n):
                pe.wait_ge(f_actd, n)
                for t in range(T):
                    for k in range(4):
                        ins = pe.transpose(ps[:, 6 + t, P * k:P * k + P], f_act[:, t, P * k:P * k + P], ident[:])
                ins.then_inc(f_tr, 1)

            def half(u, dyn, outs, h, lh, ll):
                for m in range(2):
                    unit(u + m, dyn, lh, ll, (2, CH), 4 * h + 2 * m, outs, 0, h == 0 and m == 0, h == 1 and m == 1)

            with pe.Fori(0, NF - 1) as j:
                ub, dj = b + 8, j * UPF
                pe.wait_ge(f_t1, j + 1)
                unit(ub, dj, hT_hi, hT_lo, (2, CH), 0, (0, 1), 0, True, False)
                unit(ub + 1, dj, hT_hi, hT_lo, (2, CH), 2, (0, 1), 0, False, False)
                f_turn(j + 1)
                unit(ub + 2, dj, hT_hi, hT_lo, (2, CH), 4, (0, 1), 0, False, False)
                unit(ub + 3, dj, hT_hi, hT_lo, (2, CH), 6, (0, 1), 0, False, True)
                pe.wait_ge(f_lo, j + 1)
                pe.wait_ge(f_xadd, j * 2 + 1)
                cols(ub + 4, dj, faT_hi, faT_lo, (4, 5), units=2)
                cols(ub + 6, dj, hT_hi, hT_lo, (2, 3))
                pe.wait_ge(f_xadd, j * 2 + 2)
                cols(ub + 10, dj, faT_hi, faT_lo, (4, 5), units=2)
            f_turn(NF)
            pe.wait_ge(f_lo, NF)
            pe.wait_ge(f_xadd, 2 * NF - 1)
            cols(b + 80, 0, faT_hi, faT_lo, (4, 5), units=2)
            pe.wait_ge(f_xadd, 2 * NF)
            cols(b + 82, 0, faT_hi, faT_lo, (4, 5), units=2)
            ple(0)
            attn(1)
            y = layers[1]
            x_turn(y.n2)
            pe.wait_ge(y.n2.lo, y.n2.g + 4)
            pe.wait_ge(r_w, 1)
            for t in range(T):
                for k in range(KD):
                    o = ps[:, 0, NE * t:NE * t + NE]
                    ah, al = hT_hi[:, k, P * t:P * t + P], hT_lo[:, k, P * t:P * t + P]
                    pe.matmul(o, ah, rw_hi[:, k, :], start=(k == 0), stop=False)
                    pe.matmul(o, ah, rw_lo[:, k, :], start=False, stop=False)
                    ins = pe.matmul(o, al, rw_hi[:, k, :], start=False, stop=(k == KD - 1))
            ins.then_inc(r_log, 1)
            pe.wait_ge(r_msk, 1)
            pe.matmul(ps[:, 1, 0:NE], upper[:], mask[:, 0, :], start=True, stop=True)
            pe.matmul(ps[:, 1, NE:2 * NE], upper[:], mask[:, 1, :], start=True, stop=False)
            pe.matmul(ps[:, 1, NE:2 * NE], ones[:], mask[:, 0, :], start=False, stop=True)
            pe.matmul(ps[:, 1, 2 * NE:3 * NE], ones[:], mask[:, 0, :], start=True, stop=False)
            pe.matmul(ps[:, 1, 2 * NE:3 * NE], ones[:], mask[:, 1, :], start=False, stop=True).then_inc(r_rank, 1)
            pe.wait_ge(r_np, 1)
            pe.wait_ge(hn_l, 1)
            npv = pe.value_load(npass[0:1, 0:1], min_val=1, max_val=2)
            b = FF0[1]
            with pe.Fori(0, npv) as q:
                dq = q * (UPE * NE)

                def gather(ex):
                    pe.wait_ge(e_sel, ex + 1)
                    for src, banks in ((hn_hi, (6, 7)), (hn_lo, (2, 3))):
                        for k in range(KD):
                            for t in range(T):
                                ins = pe.matmul(ps[:, banks[k // 4], P * (k % 4):P * (k % 4) + P],
                                                src[:, t, P * k:P * k + P], sel[:, t, :], start=(t == 0), stop=(t == T - 1))
                    ins.then_inc(e_gath, 1)

                def turn(ch):
                    pe.wait_ge(e_actd, ch + 1)
                    for k in range(4):
                        ins = pe.transpose(ps[:, 6, P * k:P * k + P], e_act[:, P * k:P * k + P], ident[:])
                    ins.then_inc(e_tr, 1)

                def down(u, dyn, c, first, last):
                    for m in range(2):
                        unit(u + m, dyn, eaT_hi, eaT_lo, (2, CH), 2 * m, (4 + c,), 0, first and m == 0, last and m == 1)

                def scatter(ex):
                    pe.wait_ge(e_ylo, ex * 2 + 4)
                    for t, banks in ((0, (2, 3)), (1, (6, 7))):
                        for c in range(2):
                            pe.matmul(ps[:, banks[c], :], selT[:, P * t:P * t + P], y_hi[:, CH * c:CH * c + CH], start=True, stop=False)
                            ins = pe.matmul(ps[:, banks[c], :], selT[:, P * t:P * t + P], y_lo[:, CH * c:CH * c + CH], start=False, stop=True)
                    ins.then_inc(e_scat, 1)

                def step(ub, dyn, ch, ex, fd, scat=False, sel_t=False, gath=None, new=None):
                    if new is not None:
                        pe.wait_ge(e_hsl, new + 1)
                        pe.wait_ge(e_hsh, new + 1)
                    pe.wait_ge(e_t1, ch + 1)
                    unit(ub, dyn, hs_hi, hs_lo, (2, CH), 0, (0,), 0, True, False)
                    unit(ub + 1, dyn, hs_hi, hs_lo, (2, CH), 2, (0,), 0, False, False)
                    if sel_t:
                        pe.wait_ge(e_xadd, ex * 2 + 2)
                    turn(ch)
                    unit(ub + 2, dyn, hs_hi, hs_lo, (2, CH), 4, (0,), 0, False, False)
                    unit(ub + 3, dyn, hs_hi, hs_lo, (2, CH), 6, (0,), 0, False, True)
                    pe.wait_ge(e_lo, ch)
                    if fd == 0:
                        pe.wait_ge(e_ylo, ex * 2 + (4 if scat else 2))
                    down(ub + 4, dyn, 0, fd == 0, fd == NF - 1)
                    if sel_t:
                        for t in range(T):
                            pe.transpose(ps[:, 7, P * t:P * t + P], sel[:, t, :].bitcast(F32), ident[:])
                        for t in range(T):
                            ins = pe.matmul(ps[:, 7, S:S + 1], sel[:, t, :].bitcast(F32), gcol[:, t:t + 1],
                                            start=(t == 0), stop=(t == T - 1))
                        ins.then_inc(e_st, 1)
                    if scat:
                        scatter(ex)
                    for m in range(4):
                        unit(ub + 6 + m, dyn, hs_hi, hs_lo, (2, CH), 2 * m, (1,), 0, m == 0, m == 3)
                    if gath is not None:
                        pe.wait_ge(e_stev, ex + 1)
                        gather(gath)
                    down(ub + 10, dyn, 1, fd == 0, fd == NF - 1)

                ex0 = q * NE
                pe.wait_ge(e_xadd, ex0 * 2 + 2)
                gather(ex0)
                pe.wait_ge(e_hsl, ex0 + 1)
                pe.wait_ge(e_hsh, ex0 + 1)
                ch = q * (NF * NE)
                pe.wait_ge(e_t1, ch + 1)
                for m in range(4):
                    unit(b + m, dq, hs_hi, hs_lo, (2, CH), 2 * m, (0,), 0, m == 0, m == 3)
                pe.wait_ge(e_actd, ch + 1)
                for m in range(4):
                    unit(b + 4 + m, dq, hs_hi, hs_lo, (2, CH), 2 * m, (1,), 0, m == 0, m == 3)
                step(b + 8, dq, ch + 1, ex0, 0)
                with pe.Fori(0, NE - 1) as e:
                    dyn = e * UPE + dq
                    ch0 = q * (NF * NE) + e * NF
                    ex = q * NE + e
                    for f in range(2, NF):
                        step(b + 20 + 12 * (f - 2), dyn, ch0 + f, ex, f - 1, sel_t=(f == 2),
                             gath=(ex + 1) if f == NF - 1 else None)
                    step(b + 80, dyn, ch0 + NF, ex, NF - 1, new=ex + 1)
                    step(b + 92, dyn, ch0 + NF + 1, ex, 0, scat=True)
                bl = b + UPE * (NE - 1)
                el = NE - 1
                for f in range(2, NF):
                    step(bl + 20 + 12 * (f - 2), dq, q * (NF * NE) + (el * NF + f), q * NE + el, f - 1, sel_t=(f == 2))
                chl = q * (NF * NE) + NE * NF
                turn(chl)
                pe.wait_ge(e_lo, chl)
                down(bl + 80, dq, 0, False, True)
                down(bl + 82, dq, 1, False, True)
                scatter(q * NE + el)
            ple(1, (npv - 1) * (UPE * NE))


INPUTS = ["x", "p", "positions", "attn_norm", "w_in", "q_norm", "w_uq", "kv_norm", "w_ukv", "w_br_mla", "w_br_dil",
          "w_out", "ffn_norm", "dense_w_gate", "dense_w_up", "dense_w_down", "router_w", "router_b",
          "moe_w_gate", "moe_w_up", "moe_w_down", "ple_norm", "ple_w_gate", "ple_w_proj", "final_norm"]


def kernel(**inputs):
    import concourse.bacc as bacc
    from concourse.bass_utils import run_bass_kernel_spmd

    nc = bacc.Bacc("TRN2", target_bir_lowering=False, num_devices=1)
    arrays, args = {}, []
    for name in INPUTS:
        a = np.ascontiguousarray(inputs[name])
        arrays[f"in_{name}"] = a
        args.append(nc.dram_tensor(f"in_{name}", a.shape, mybir.dt.from_np(a.dtype), kind="ExternalInput").ap())
    args.append(nc.dram_tensor("out_x", (1, S, D), F32, kind="ExternalOutput").ap())
    trunk_kernel(nc, *args)
    r = run_bass_kernel_spmd(nc, [arrays], core_ids=[0])
    return r.results[0]["out_x"]
```
